# Optimizing a Trainium2 kernel written in Bass

```python
import jax
import jax.numpy as jnp
from jax import lax
import numpy as np

D_MODEL = 1024
BATCH = 1
SEQ = 1024
DEPTH = 2
DEC_BATCH = 8
DEC_SEQ = 4
PAST_LEN = 1024
PAGE_SIZE = 128

N_MIXERS = 2
N_SWA_LAYERS = (DEPTH + 1) // 2
N_MLA_LAYERS = DEPTH // 2

SWA_HEADS = 16
SWA_KV_HEADS = 4
SWA_GROUP = SWA_HEADS // SWA_KV_HEADS
SWA_HEAD_DIM = 64
WINDOW = 128
SWA_BLOCK = WINDOW

MLA_HEADS = 16
MLA_Q_LORA = 384
MLA_KV_LORA = 256
MLA_NOPE = 64
MLA_ROPE = 32
MLA_V = 64
MLA_Q_BLOCK = 128
ROPE_THETA = 10000.0

N_GROUPS = 8
EXPERTS_PER_GROUP = 8
N_EXPERTS = N_GROUPS * EXPERTS_PER_GROUP
TOP_K = 2
D_EXPERT = 256
MOE_BLOCK = 128

RMS_EPS = 1e-6
NEG_INF = -1e30

kernel_name = 'hybrid_swa_mla_hmoe_step'

def rms_norm(x, g):
    xf = x.astype(jnp.float32)
    y = xf * lax.rsqrt(jnp.mean(xf * xf, axis=-1, keepdims=True) + RMS_EPS)
    return (y * g.astype(jnp.float32)).astype(x.dtype)

def apply_rope(x, pos):
    half = MLA_ROPE // 2
    inv = jnp.power(ROPE_THETA, -jnp.arange(half, dtype=jnp.float32) * 2.0 / MLA_ROPE)
    ang = pos[:, None] * inv[None, :]
    shape = (1, ang.shape[0]) + (1,) * (x.ndim - 3) + (half,)
    cos = jnp.cos(ang).reshape(shape)
    sin = jnp.sin(ang).reshape(shape)
    xf = x.astype(jnp.float32)
    x1, x2 = xf[..., :half], xf[..., half:]
    return jnp.concatenate([x1 * cos - x2 * sin, x2 * cos + x1 * sin], axis=-1).astype(x.dtype)

def alibi_slopes():
    h = jnp.arange(1, SWA_HEADS + 1, dtype=jnp.float32)
    return jnp.exp2(-8.0 * h / SWA_HEADS).reshape(SWA_KV_HEADS, SWA_GROUP)

def sink_softmax(scores, sinks):
    m = jnp.maximum(jnp.max(scores, axis=-1, keepdims=True), sinks)
    p = jnp.exp(scores - m)
    return p / (jnp.sum(p, axis=-1, keepdims=True) + jnp.exp(sinks - m))

def swa_qkv(h, w_qkv, b_qkv):
    b, s, _ = h.shape
    nq = SWA_HEADS * SWA_HEAD_DIM
    nk = SWA_KV_HEADS * SWA_HEAD_DIM
    qkv = h @ w_qkv + b_qkv
    q = qkv[..., :nq].reshape(b, s, SWA_KV_HEADS, SWA_GROUP, SWA_HEAD_DIM)
    k = qkv[..., nq:nq + nk].reshape(b, s, SWA_KV_HEADS, SWA_HEAD_DIM)
    v = qkv[..., nq + nk:].reshape(b, s, SWA_KV_HEADS, SWA_HEAD_DIM)
    return q, k, v

def swa_prompt(h, w_qkv, b_qkv, sinks, w_o, b_o):
    b, s, _ = h.shape
    nb = s // SWA_BLOCK
    scale = SWA_HEAD_DIM ** -0.5
    q, k, v = swa_qkv(h, w_qkv, b_qkv)
    qb = q.reshape(b, nb, SWA_BLOCK, SWA_KV_HEADS, SWA_GROUP, SWA_HEAD_DIM)
    kb = k.reshape(b, nb, SWA_BLOCK, SWA_KV_HEADS, SWA_HEAD_DIM)
    vb = v.reshape(b, nb, SWA_BLOCK, SWA_KV_HEADS, SWA_HEAD_DIM)
    pad = jnp.zeros_like(kb[:, :1])
    kk = jnp.concatenate([jnp.concatenate([pad, kb[:, :-1]], axis=1), kb], axis=2)
    vv = jnp.concatenate([jnp.concatenate([pad, vb[:, :-1]], axis=1), vb], axis=2)
    sc = jnp.einsum('bnqkgd,bnskd->bnkgqs', qb, kk, preferred_element_type=jnp.float32) * scale
    qi = jnp.arange(SWA_BLOCK)[:, None]
    kj = jnp.arange(2 * SWA_BLOCK)[None, :]
    dist = qi + SWA_BLOCK - kj
    kpos = jnp.arange(nb)[:, None, None] * SWA_BLOCK + kj[None] - SWA_BLOCK
    valid = (dist >= 0) & (dist < WINDOW) & (kpos >= 0)
    bias = -alibi_slopes()[:, :, None, None] * dist.astype(jnp.float32)
    sc = jnp.where(valid[None, :, None, None], sc + bias, NEG_INF)
    p = sink_softmax(sc, sinks.astype(jnp.float32).reshape(SWA_KV_HEADS, SWA_GROUP)[:, :, None, None])
    o = jnp.einsum('bnkgqs,bnskd->bnqkgd', p.astype(vv.dtype), vv)
    y = o.reshape(b, s, SWA_HEADS * SWA_HEAD_DIM) @ w_o + b_o
    return y, k[:, s - WINDOW:], v[:, s - WINDOW:]

def swa_sample(h, buf_k, buf_v, w_qkv, b_qkv, sinks, w_o, b_o):
    b, t, _ = h.shape
    scale = SWA_HEAD_DIM ** -0.5
    q, k, v = swa_qkv(h, w_qkv, b_qkv)
    kk = jnp.concatenate([buf_k, k], axis=1)
    vv = jnp.concatenate([buf_v, v], axis=1)
    sc = jnp.einsum('btkgd,bskd->bkgts', q, kk, preferred_element_type=jnp.float32) * scale
    dist = (WINDOW + jnp.arange(t))[:, None] - jnp.arange(WINDOW + t)[None, :]
    valid = (dist >= 0) & (dist < WINDOW)
    bias = -alibi_slopes()[:, :, None, None] * dist.astype(jnp.float32)
    sc = jnp.where(valid, sc + bias, NEG_INF)
    p = sink_softmax(sc, sinks.astype(jnp.float32).reshape(SWA_KV_HEADS, SWA_GROUP)[:, :, None, None])
    o = jnp.einsum('bkgts,bskd->btkgd', p.astype(vv.dtype), vv)
    y = o.reshape(b, t, SWA_HEADS * SWA_HEAD_DIM) @ w_o + b_o
    return y, kk[:, t:], vv[:, t:]

def mla_project(h, pos, w_dqkv, norm_q, norm_kv, w_uq):
    b, s, _ = h.shape
    a = h @ w_dqkv
    cq = rms_norm(a[..., :MLA_Q_LORA], norm_q)
    c = rms_norm(a[..., MLA_Q_LORA:MLA_Q_LORA + MLA_KV_LORA], norm_kv)
    kr = apply_rope(a[..., MLA_Q_LORA + MLA_KV_LORA:], pos)
    q = (cq @ w_uq).reshape(b, s, MLA_HEADS, MLA_NOPE + MLA_ROPE)
    qn = q[..., :MLA_NOPE]
    qr = apply_rope(q[..., MLA_NOPE:], pos)
    return qn, qr, c, kr

def mla_prompt(h, w_dqkv, norm_q, norm_kv, w_uq, w_uk, w_uv, w_o):
    b, s, _ = h.shape
    scale = (MLA_NOPE + MLA_ROPE) ** -0.5
    qn, qr, c, kr = mla_project(h, jnp.arange(s, dtype=jnp.float32), w_dqkv, norm_q, norm_kv, w_uq)
    kn = jnp.einsum('bsc,chd->bshd', c, w_uk)
    v = jnp.einsum('bsc,chd->bshd', c, w_uv)
    nb = s // MLA_Q_BLOCK
    qn_b = qn.reshape(b, nb, MLA_Q_BLOCK, MLA_HEADS, MLA_NOPE).transpose(1, 0, 2, 3, 4)
    qr_b = qr.reshape(b, nb, MLA_Q_BLOCK, MLA_HEADS, MLA_ROPE).transpose(1, 0, 2, 3, 4)
    kpos = jnp.arange(s)

    def q_block(args):
        qn_i, qr_i, n = args
        sc = (jnp.einsum('bqhd,bshd->bhqs', qn_i, kn, preferred_element_type=jnp.float32)
              + jnp.einsum('bqhr,bsr->bhqs', qr_i, kr, preferred_element_type=jnp.float32)) * scale
        qpos = n * MLA_Q_BLOCK + jnp.arange(MLA_Q_BLOCK)
        sc = jnp.where(kpos[None, :] <= qpos[:, None], sc, NEG_INF)
        p = jax.nn.softmax(sc, axis=-1)
        return jnp.einsum('bhqs,bshd->bqhd', p.astype(v.dtype), v)

    o = lax.map(q_block, (qn_b, qr_b, jnp.arange(nb)))
    y = o.transpose(1, 0, 2, 3, 4).reshape(b, s, MLA_HEADS * MLA_V) @ w_o
    return y, c, kr

def mla_sample(h, cache_c, cache_r, page_table, w_dqkv, norm_q, norm_kv, w_uq, w_uk, w_uv, w_o):
    b, t, _ = h.shape
    scale = (MLA_NOPE + MLA_ROPE) ** -0.5
    pos = PAST_LEN + jnp.arange(t, dtype=jnp.float32)
    qn, qr, c, kr = mla_project(h, pos, w_dqkv, norm_q, norm_kv, w_uq)
    past_c = cache_c[page_table].reshape(b, -1, MLA_KV_LORA)
    past_r = cache_r[page_table].reshape(b, -1, MLA_ROPE)
    n_past = past_c.shape[1]
    q_lat = jnp.einsum('bthd,chd->bthc', qn, w_uk)
    s_past = (jnp.einsum('bthc,bsc->bhts', q_lat, past_c, preferred_element_type=jnp.float32)
              + jnp.einsum('bthr,bsr->bhts', qr, past_r, preferred_element_type=jnp.float32)) * scale
    s_new = (jnp.einsum('bthc,bsc->bhts', q_lat, c, preferred_element_type=jnp.float32)
             + jnp.einsum('bthr,bsr->bhts', qr, kr, preferred_element_type=jnp.float32)) * scale
    causal = jnp.arange(t)[None, :] <= jnp.arange(t)[:, None]
    s_new = jnp.where(causal, s_new, NEG_INF)
    p = jax.nn.softmax(jnp.concatenate([s_past, s_new], axis=-1), axis=-1).astype(c.dtype)
    o_lat = (jnp.einsum('bhts,bsc->bthc', p[..., :n_past], past_c)
             + jnp.einsum('bhts,bsc->bthc', p[..., n_past:], c))
    o = jnp.einsum('bthc,chd->bthd', o_lat, w_uv)
    y = o.reshape(b, t, MLA_HEADS * MLA_V) @ w_o
    return y, c, kr

def hier_moe(x, w_group, b_group, w_expert, b_expert, w_gate, w_up, w_down):
    n_tok, d = x.shape
    xf = x.astype(jnp.float32)
    g_logits = xf @ w_group.astype(jnp.float32) + b_group.astype(jnp.float32)
    g_prob = jax.nn.softmax(g_logits, axis=-1)
    g_idx = jnp.argmax(g_logits, axis=-1)
    g_gate = jnp.take_along_axis(g_prob, g_idx[:, None], axis=-1)
    e_logits = (xf @ w_expert.astype(jnp.float32) + b_expert.astype(jnp.float32)).reshape(n_tok, N_GROUPS, EXPERTS_PER_GROUP)
    e_in = jnp.take_along_axis(e_logits, g_idx[:, None, None], axis=1)[:, 0]
    e_val, e_idx = lax.top_k(e_in, TOP_K)
    gates = jax.nn.softmax(e_val, axis=-1) * g_gate
    expert_id = g_idx[:, None] * EXPERTS_PER_GROUP + e_idx
    n_asg = n_tok * TOP_K
    flat_e = expert_id.reshape(n_asg)
    order = jnp.argsort(flat_e)
    sorted_e = flat_e[order]
    tok = order // TOP_K
    counts = jnp.bincount(flat_e, length=N_EXPERTS)
    padded = (counts + MOE_BLOCK - 1) // MOE_BLOCK * MOE_BLOCK
    start = jnp.cumsum(counts) - counts
    pend = jnp.cumsum(padded)
    pstart = pend - padded
    dest = pstart[sorted_e] + jnp.arange(n_asg) - start[sorted_e]
    n_blocks = -(-n_asg // MOE_BLOCK) + N_EXPERTS
    buf = jnp.zeros((n_blocks * MOE_BLOCK, d), x.dtype).at[dest].set(x[tok])
    blk_e = jnp.minimum(jnp.searchsorted(pend, jnp.arange(n_blocks) * MOE_BLOCK, side='right'), N_EXPERTS - 1)

    def expert_block(args):
        xb, e = args
        hb = jax.nn.silu(xb @ w_gate[e]) * (xb @ w_up[e])
        return hb @ w_down[e]

    yb = lax.map(expert_block, (buf.reshape(n_blocks, MOE_BLOCK, d), blk_e)).reshape(n_blocks * MOE_BLOCK, d)
    y_sorted = yb[dest] * gates.reshape(n_asg)[order][:, None].astype(x.dtype)
    return jnp.zeros_like(x).at[tok].add(y_sorted)

def setup_inputs(seed: int = 0) -> dict:
    key = jax.random.key(seed)
    ks = jax.random.split(key, 32)
    f32 = jnp.float32
    n_pages = PAST_LEN // PAGE_SIZE
    n_used = DEC_BATCH * n_pages
    n_pool = n_used + max(1, n_used // 4)

    def nrm(k, shape, scale):
        return jax.random.normal(k, shape, f32) * scale

    def gain(k, shape):
        return 1.0 + nrm(k, shape, 0.05)

    qkv_width = (SWA_HEADS + 2 * SWA_KV_HEADS) * SWA_HEAD_DIM
    dqkv_width = MLA_Q_LORA + MLA_KV_LORA + MLA_ROPE
    page_table = jax.random.permutation(ks[6], n_pool)[:n_used].reshape(DEC_BATCH, n_pages).astype(jnp.int32)
    return {
        'x_prompt': nrm(ks[0], (BATCH, SEQ, D_MODEL), 1.0),
        'x_sample': nrm(ks[1], (DEC_BATCH, DEC_SEQ, D_MODEL), 1.0),
        'cache_swa_k': nrm(ks[2], (N_SWA_LAYERS, DEC_BATCH, WINDOW, SWA_KV_HEADS, SWA_HEAD_DIM), 1.0),
        'cache_swa_v': nrm(ks[3], (N_SWA_LAYERS, DEC_BATCH, WINDOW, SWA_KV_HEADS, SWA_HEAD_DIM), 1.0),
        'cache_mla_latent': nrm(ks[4], (N_MLA_LAYERS, n_pool, PAGE_SIZE, MLA_KV_LORA), 1.0),
        'cache_mla_krope': nrm(ks[5], (N_MLA_LAYERS, n_pool, PAGE_SIZE, MLA_ROPE), 1.0),
        'page_table': page_table,
        'norm_attn': gain(ks[7], (DEPTH, D_MODEL)),
        'norm_ffn': gain(ks[8], (DEPTH, D_MODEL)),
        'norm_final': gain(ks[9], (D_MODEL,)),
        'swa_w_qkv': nrm(ks[10], (N_SWA_LAYERS, D_MODEL, qkv_width), D_MODEL ** -0.5),
        'swa_b_qkv': nrm(ks[11], (N_SWA_LAYERS, qkv_width), 0.02),
        'swa_sinks': nrm(ks[12], (N_SWA_LAYERS, SWA_HEADS), 0.5),
        'swa_w_o': nrm(ks[13], (N_SWA_LAYERS, SWA_HEADS * SWA_HEAD_DIM, D_MODEL), (SWA_HEADS * SWA_HEAD_DIM) ** -0.5),
        'swa_b_o': nrm(ks[14], (N_SWA_LAYERS, D_MODEL), 0.02),
        'mla_w_dqkv': nrm(ks[15], (N_MLA_LAYERS, D_MODEL, dqkv_width), D_MODEL ** -0.5),
        'mla_norm_q': gain(ks[16], (N_MLA_LAYERS, MLA_Q_LORA)),
        'mla_norm_kv': gain(ks[17], (N_MLA_LAYERS, MLA_KV_LORA)),
        'mla_w_uq': nrm(ks[18], (N_MLA_LAYERS, MLA_Q_LORA, MLA_HEADS * (MLA_NOPE + MLA_ROPE)), MLA_Q_LORA ** -0.5),
        'mla_w_uk': nrm(ks[19], (N_MLA_LAYERS, MLA_KV_LORA, MLA_HEADS, MLA_NOPE), MLA_KV_LORA ** -0.5),
        'mla_w_uv': nrm(ks[20], (N_MLA_LAYERS, MLA_KV_LORA, MLA_HEADS, MLA_V), MLA_KV_LORA ** -0.5),
        'mla_w_o': nrm(ks[21], (N_MLA_LAYERS, MLA_HEADS * MLA_V, D_MODEL), (MLA_HEADS * MLA_V) ** -0.5),
        'moe_w_group': nrm(ks[22], (DEPTH, D_MODEL, N_GROUPS), D_MODEL ** -0.5),
        'moe_b_group': nrm(ks[23], (DEPTH, N_GROUPS), 0.01),
        'moe_w_expert': nrm(ks[24], (DEPTH, D_MODEL, N_EXPERTS), D_MODEL ** -0.5),
        'moe_b_expert': nrm(ks[25], (DEPTH, N_EXPERTS), 0.01),
        'moe_w_gate': nrm(ks[26], (DEPTH, N_EXPERTS, D_MODEL, D_EXPERT), D_MODEL ** -0.5),
        'moe_w_up': nrm(ks[27], (DEPTH, N_EXPERTS, D_MODEL, D_EXPERT), D_MODEL ** -0.5),
        'moe_w_down': nrm(ks[28], (DEPTH, N_EXPERTS, D_EXPERT, D_MODEL), D_EXPERT ** -0.5),
    }

def reference(x_prompt, x_sample, cache_swa_k, cache_swa_v, cache_mla_latent, cache_mla_krope, page_table,
              norm_attn, norm_ffn, norm_final,
              swa_w_qkv, swa_b_qkv, swa_sinks, swa_w_o, swa_b_o,
              mla_w_dqkv, mla_norm_q, mla_norm_kv, mla_w_uq, mla_w_uk, mla_w_uv, mla_w_o,
              moe_w_group, moe_b_group, moe_w_expert, moe_b_expert, moe_w_gate, moe_w_up, moe_w_down):
    xp, xs = x_prompt, x_sample
    swa_kp, swa_vp, swa_ks, swa_vs = [], [], [], []
    mla_cp, mla_rp, mla_cs, mla_rs = [], [], [], []
    for i in range(DEPTH):
        j = i // N_MIXERS
        hp = rms_norm(xp, norm_attn[i])
        hs = rms_norm(xs, norm_attn[i])
        if i % N_MIXERS == 0:
            ap, kp, vp = swa_prompt(hp, swa_w_qkv[j], swa_b_qkv[j], swa_sinks[j], swa_w_o[j], swa_b_o[j])
            a_s, k_s, v_s = swa_sample(hs, cache_swa_k[j], cache_swa_v[j], swa_w_qkv[j], swa_b_qkv[j],
                                       swa_sinks[j], swa_w_o[j], swa_b_o[j])
            swa_kp.append(kp)
            swa_vp.append(vp)
            swa_ks.append(k_s)
            swa_vs.append(v_s)
        else:
            ap, cp, rp = mla_prompt(hp, mla_w_dqkv[j], mla_norm_q[j], mla_norm_kv[j], mla_w_uq[j],
                                    mla_w_uk[j], mla_w_uv[j], mla_w_o[j])
            a_s, c_s, r_s = mla_sample(hs, cache_mla_latent[j], cache_mla_krope[j], page_table,
                                       mla_w_dqkv[j], mla_norm_q[j], mla_norm_kv[j], mla_w_uq[j],
                                       mla_w_uk[j], mla_w_uv[j], mla_w_o[j])
            mla_cp.append(cp)
            mla_rp.append(rp)
            mla_cs.append(c_s)
            mla_rs.append(r_s)
        xp = xp + ap
        xs = xs + a_s
        fp = rms_norm(xp, norm_ffn[i])
        fs = rms_norm(xs, norm_ffn[i])
        n_p = fp.shape[0] * fp.shape[1]
        tokens = jnp.concatenate([fp.reshape(-1, D_MODEL), fs.reshape(-1, D_MODEL)], axis=0)
        f = hier_moe(tokens, moe_w_group[i], moe_b_group[i], moe_w_expert[i], moe_b_expert[i],
                     moe_w_gate[i], moe_w_up[i], moe_w_down[i])
        xp = xp + f[:n_p].reshape(xp.shape)
        xs = xs + f[n_p:].reshape(xs.shape)
    y_prompt = rms_norm(xp, norm_final)
    y_sample = rms_norm(xs, norm_final)
    return (y_prompt, y_sample,
            jnp.stack(swa_kp), jnp.stack(swa_vp), jnp.stack(swa_ks), jnp.stack(swa_vs),
            jnp.stack(mla_cp), jnp.stack(mla_rp), jnp.stack(mla_cs), jnp.stack(mla_rs))


_drawn_inputs = setup_inputs


def setup_inputs(seed=0):
    import zlib

    import numpy as np

    out = dict(_drawn_inputs(seed))
    spreads = {}
    factors = {'mla_norm_q': 4.674, 'moe_b_group': 4.331, 'moe_b_expert': 3.25}
    for name, (base, spread) in spreads.items():
        noise = np.random.default_rng([zlib.crc32(name.encode()), seed]).standard_normal(out[name].shape)
        drawn = base * np.exp(spread * noise) if base else spread * noise
        out[name] = jnp.asarray(drawn.astype(out[name].dtype))
    for name, factor in factors.items():
        out[name] = (out[name] * factor).astype(out[name].dtype)
    return out
```

```python
from contextlib import ExitStack

import numpy as np

import concourse.bass as bass
from concourse import mybir

F32 = mybir.dt.float32
I32 = mybir.dt.int32
ACT = mybir.ActivationFunctionType
ALU = mybir.AluOpType
AX = mybir.AxisListType

P = 128
D = 1024
SEQ = 1024
NB = 8
NT = 4
NS = NB * NT
PT = SEQ // P
TILES = PT + 1
ROWS = TILES * P
KC = D // P
HEADS = 16
KVH = 4
GRP = HEADS // KVH
HD = 64
WIN = 128
QKV = (HEADS + 2 * KVH) * HD
KVW = KVH * HD
QL = 384
KVL = 256
NOPE = 64
ROPE = 32
QD = NOPE + ROPE
DQ = QL + KVL + ROPE
PAGE = 128
PAGES = 8
NG = 8
EPG = 8
NE = NG * EPG
DE = 256
MAXOV = 16
NCOL = NE + MAXOV
EPS = 1e-6
NEG = -1e30
SLOPES = [2.0 ** (-8.0 * h / HEADS) for h in range(1, HEADS + 1)]
PAD_ROW = 4096


def shape_constants():
    q = np.arange(P)[:, None]
    k = np.arange(2 * WIN)[None, :]
    dist = q + WIN - k
    ok = (dist >= 0) & (dist < WIN)
    later = np.where(ok, -dist, NEG)
    first = np.where(ok & (k >= WIN), -dist, NEG)
    sb = np.zeros((P, WIN + NT))
    for g in range(KVH):
        for j in range(GRP):
            for t in range(NT):
                dd = WIN + t - np.arange(WIN + NT)
                sb[32 * g + 4 * j + t] = np.where((dd >= 0) & (dd < WIN), -SLOPES[GRP * g + j] * dd, NEG)
    causal = np.where(np.arange(P)[None, :] <= q, 0.0, NEG)
    scausal = np.where(np.arange(NT)[None, :] <= (np.arange(HEADS * NT) % NT)[:, None], 0.0, NEG)
    pos = np.zeros((TILES, P), np.float32)
    pos[:PT] = np.arange(SEQ).reshape(PT, P)
    pos[PT, :NS] = SEQ + np.arange(NS) % NT
    inv = np.power(np.float32(10000.0), -np.arange(ROPE // 2, dtype=np.float32) * np.float32(2.0) / np.float32(ROPE))
    ang = (pos[:, :, None] * inv.astype(np.float32)).astype(np.float32).astype(np.float64)
    rope = np.stack([np.cos(ang), np.sin(ang)], axis=2)
    valid = np.ones((P, TILES))
    valid[NS:, PT] = 0.0
    aid = (np.arange(TILES)[None, :] * P + q) * 2.0 + 1.0
    f = lambda a: np.ascontiguousarray(a, dtype=np.float32)
    return {
        "c_ident": f(np.eye(P)),
        "c_before": f(np.arange(P)[:, None] < np.arange(P)[None, :]),
        "c_iota": f(np.broadcast_to(np.arange(P), (P, P))),
        "c_swa_dist": f(np.stack([first, later], axis=1)),
        "c_swa_sample_bias": f(sb),
        "c_causal": f(causal),
        "c_sample_causal": f(scausal),
        "c_rope": f(rope.transpose(1, 0, 2, 3)),
        "c_valid": f(valid),
        "c_aid": f(aid),
        "c_rank": f(np.broadcast_to(EPG - np.arange(EPG), (P, EPG))),
    }


def over_tiles(eng, body):
    body(0, 0, False)
    body(1, 1, False)
    with eng.Fori(2, PT - 1, 2) as t:
        body(t, 0, False)
        body(t + 1, 1, False)
    body(PT, 0, True)


def nth(t, s):
    return (t - s + 2) * 8


def wait_if(eng, sem, n):
    if not isinstance(n, int) or n > 0:
        eng.wait_ge(sem, n)


def wait_apart(eng, sem, n, passed):
    eng.wait_ge(sem, n)
    eng.sem_inc(passed, 1)


class Chain:

    def __init__(self, eng, sem, per_tile=0):
        self.eng, self.sem, self.per_tile, self.base, self.n = eng, sem, per_tile, 0, 0

    def tile(self, t):
        self.base, self.n = t * self.per_tile, 0

    def link(self, ins):
        self.n += 1
        ins.then_inc(self.sem, 1)
        self.eng.wait_ge(self.sem, self.base + self.n)


def permuted(ap):
    return ap.rearrange("p (c j) -> p j c", c=KC)


def natural(ap):
    return ap.rearrange("p (j c) -> p j c", c=KC)


class Phase:

    def __init__(self, nc, stack, tag):
        self.nc, self.stack, self.tag, self.taken = nc, stack, tag, []
        stack.callback(self.release)

    def release(self):
        if self.taken:
            self.nc.clear_and_free_semaphores(self.taken)
            self.nc.all_engine_barrier()

    def sb(self, name, shape, dt=F32):
        return self.stack.enter_context(self.nc.sbuf_tensor(self.tag + name, shape, dt))

    def ps(self, name, shape, dt=F32):
        return self.stack.enter_context(self.nc.psum_tensor(self.tag + name, shape, dt))

    def sem(self, name):
        self.taken.append(self.nc.alloc_semaphore(self.tag + name))
        return self.taken[-1]

    def sems(self, name, n):
        return [self.sem(f"{name}{i}") for i in range(n)]


def setup_phase(nc, io, dram, cst):
    with ExitStack() as stack:
        c = Phase(nc, stack, "s_")
        zeros = c.sb("zeros", [P, 2 * D])
        loaded, zeroed, stored = c.sem("loaded"), c.sem("zeroed"), c.sem("stored")
        block = stack.enter_context(nc.Block())

        @block.sync
        def _(eng):
            names = ["ident", "before", "iota", "causal", "rope", "valid", "aid", "rank"]
            for n in names:
                eng.dma_start(cst[n][:], io["c_" + n]).then_inc(loaded, 16)
            eng.wait_ge(loaded, 16 * len(names))

        @block.scalar
        def _(eng):
            eng.wait_ge(zeroed, 1)
            pad = P - NS
            y = dram["expert_rows"].rearrange("(t k) d -> t (k d)", k=2)
            eng.dma_start(y[SEQ + NS:ROWS, :], zeros[0:pad, :]).then_inc(stored, 16)
            eng.dma_start(dram["x0"][NS:P, :], zeros[0:pad, 0:D]).then_inc(stored, 16)
            eng.dma_start(dram["x0"][0:NS, :], io["x_sample"].rearrange("b t d -> (b t) d")).then_inc(stored, 16)
            eng.wait_ge(stored, 48)

        @block.vector
        def _(eng):
            eng.memset(zeros[:], 0.0).then_inc(zeroed, 1)
            eng.memset(cst["ones"][:], 1.0).then_inc(zeroed, 1)


def swa_attention_phase(nc, io, dram, cst, o_all):
    ident = cst["ident"]
    PAIRS = HEADS // 2

    def head(i, j):
        return GRP * (i // 2) + 2 * j + i % 2

    with ExitStack() as stack:
        c = Phase(nc, stack, "a_")
        gain = c.sb("gain", [P, D])
        bias = c.sb("bias", [P, QKV])
        sink = c.sb("sink", [P, HEADS])
        nsink = c.sb("nsink", [P, HEADS])
        q = c.sb("q", [P, D])
        kv = c.sb("kv", [P, 2, 2 * KVW])
        ps_t = c.ps("ps_t", [P, D])
        ps_q = c.ps("ps_q", [P, 2, 512])
        ps_s = c.ps("ps_s", [P, 2, 2, 2 * WIN])
        ps_p = c.ps("ps_p", [P, 4, P])
        ps_o = c.ps("ps_o", [P, HEADS // 2, HD])

        with ExitStack() as inner:
            c = Phase(nc, inner, "a_")
            w = c.sb("w", [P, KC, QKV])
            dist = c.sb("dist", [P, 2, 2 * WIN])
            x = c.sb("x", [P, 2, D])
            junk = c.sb("junk", [P, D])
            ss, ms, rms, rstd = (c.sb(n, [P, 2, 1]) for n in ("ss", "ms", "rms", "rstd"))
            h = c.sb("h", [P, D])
            hT = c.sb("hT", [P, KC, P])
            kdup = c.sb("kdup", [P, KVH, 2, HD])
            qT = c.sb("qT", [P, KC, P])
            kT = c.sb("kT", [P, 2, KVH, P])
            s = c.sb("s", [P, 2, 2, 2 * WIN])
            p = c.sb("p", [P, 2, 2, 2 * WIN])
            pT = c.sb("pT", [P, 2, 4, P])
            nm, den, tmp, esink = (c.sb(n, [P, HEADS]) for n in ("nm", "den", "tmp", "esink"))

            w_in, small_in = c.sems("w_in", 3), c.sem("small_in")
            x_in = c.sems("x_in", 2)
            sq_done, ms_done, rms_done, h_done = (c.sem(n) for n in ("sq_done", "ms_done", "rms_done", "h_done"))
            hT_made, hT_done = c.sem("hT_made"), c.sem("hT_done")
            qkv_made, qkv_done, kdup_done = c.sem("qkv_made"), c.sem("qkv_done"), c.sem("kdup_done")
            qkT_made, qkT_done = c.sem("qkT_made"), c.sem("qkT_done")
            s_made, s_done, p_done = c.sem("s_made"), c.sem("s_done"), c.sem("p_done")
            pT_made, pT_done, o_made, o_done = (c.sem(n) for n in ("pT_made", "pT_done", "o_made", "o_done"))
            es_in, es_done = c.sem("es_in"), c.sem("es_done")
            chain, kv_out = c.sem("chain"), c.sem("kv_out")
            block = inner.enter_context(nc.Block())

            @block.sync
            def _(eng):
                xp = io["x_prompt"][0].rearrange("(t p) d -> t p d", p=P)
                eng.dma_start(x[:, 0, :], xp[0]).then_inc(x_in[0], 16)
                wv = io["swa_w_qkv"][0].rearrange("(p c) n -> p c n", c=KC)
                for n in range(3):
                    for k in range(0, KC, 2):
                        cols = slice(512 * n, 512 * n + 512)
                        eng.dma_start(w[:, k:k + 2, cols], wv[:, k:k + 2, cols]).then_inc(w_in[n], 16)
                eng.dma_start(x[:, 1, :], xp[1]).then_inc(x_in[1], 16)
                with eng.Fori(2, PT - 1, 2) as t:
                    for sl in range(2):
                        eng.wait_ge(h_done, t + sl - 1)
                        eng.dma_start(x[:, sl, :], xp[t + sl]).then_inc(x_in[sl], 16)
                eng.wait_ge(h_done, PT - 1)
                eng.dma_start(x[:, 0, :], dram["x0"][:]).then_inc(x_in[0], 16)
                eng.wait_ge(qkv_done, 3 * PT)
                eng.dma_start(io["o_swa_k_prompt"][0, 0].rearrange("w g d -> w (g d)"), kv[:, 1, 0:KVW]).then_inc(kv_out, 16)
                eng.dma_start(io["o_swa_v_prompt"][0, 0].rearrange("w g d -> w (g d)"), kv[:, 1, KVW:]).then_inc(kv_out, 16)
                eng.wait_ge(kv_out, 32)

            @block.scalar
            def _(eng):
                eng.dma_start(gain[:], io["norm_attn"][0:1, :].partition_broadcast(P)).then_inc(small_in, 16)
                eng.dma_start(bias[:], io["swa_b_qkv"].partition_broadcast(P)).then_inc(small_in, 16)
                eng.dma_start(sink[:], io["swa_sinks"].partition_broadcast(P)).then_inc(small_in, 16)
                eng.dma_start(dist[:], io["c_swa_dist"]).then_inc(small_in, 16)

                def norm(t, sl):
                    eng.wait_ge(x_in[sl], nth(t, sl))
                    wait_if(eng, sq_done, t)
                    eng.activation(junk[:], x[:, sl, :], ACT.Square, accum_out=ss[:, sl, :]).then_inc(sq_done, 1)
                    eng.wait_ge(ms_done, t + 1)
                    eng.activation(rms[:, sl, :], ms[:, sl, :], ACT.Sqrt).then_inc(rms_done, 1)

                def hT_out(t):
                    eng.wait_ge(hT_made, t + 1)
                    eng.copy(hT[:], ps_t[:].rearrange("p (c j) -> p c j", c=KC)).then_inc(hT_done, 1)

                norm(0, 0)
                hT_out(0)

                def body(t, sl, last):
                    if last:
                        return
                    eng.wait_ge(qkv_done, 3 * t + 3)
                    k4 = kv[:, sl, 0:KVW].rearrange("p (g d) -> p g d", g=KVH)
                    for a in range(2):
                        eng.copy(kdup[:, :, a, :], k4).then_inc(kdup_done, 1)
                    norm(t + 1, 1 - sl)
                    eng.wait_ge(qkT_made, 2 * t + 1)
                    eng.copy(qT[:], ps_t[:].rearrange("p (c j) -> p c j", c=KC)).then_inc(qkT_done, 1)
                    eng.wait_ge(qkT_made, 2 * t + 2)
                    eng.copy(kT[:, sl], ps_p[:]).then_inc(qkT_done, 1)

                    def exps(i):
                        n = PAIRS * t + i
                        eng.wait_ge(s_done, n + 1)
                        wait_if(eng, pT_made, n - 1)
                        if i % 4 == 0:
                            wait_if(eng, o_done, 2 * t + i // 4 - 1)
                        for j in range(2):
                            hh = head(i, j)
                            ins = eng.activation(p[:, i % 2, j, :], s[:, i % 2, j, :], ACT.Exp,
                                                 bias=nm[:, hh:hh + 1], accum_out=den[:, hh:hh + 1])
                            ins.then_inc(p_done, 1)

                    def pT_out(i):
                        n = PAIRS * t + i
                        eng.wait_ge(pT_made, n + 1)
                        wait_if(eng, o_made, n - 1)
                        eng.copy(pT[:, i % 2], ps_p[:]).then_inc(pT_done, 1)

                    def exp_sinks(half):
                        eng.wait_ge(es_in, 2 * t + half + 1)
                        a = half * 8
                        eng.activation(esink[:, a:a + 8], tmp[:, a:a + 8], ACT.Exp).then_inc(es_done, 1)

                    for i in range(PAIRS):
                        exps(i)
                        if i == 0:
                            hT_out(t + 1)
                        if i:
                            pT_out(i - 1)
                        if i == 4:
                            exp_sinks(0)
                    exp_sinks(1)
                    pT_out(PAIRS - 1)
                over_tiles(eng, body)

            @block.vector
            def _(eng):
                STEPS = 1 + 2 * PAIRS + 2 * PAIRS + 6
                ch = Chain(eng, chain, STEPS)
                eng.memset(kT[:, 1], 0.0).then_inc(chain, 1)
                eng.memset(kv[:, 1, :], 0.0).then_inc(chain, 1)
                eng.wait_ge(small_in, 64)
                eng.tensor_scalar(nsink[:], sink[:], -1.0, None, ALU.mult).then_inc(chain, 1)
                eng.tensor_scalar(bias[:, 0:D], bias[:, 0:D], HD ** -0.5, None, ALU.mult).then_inc(chain, 1)
                eng.wait_ge(chain, 4)

                def norm(t, sl):
                    eng.wait_ge(sq_done, t + 1)
                    eng.tensor_scalar(ms[:, sl, :], ss[:, sl, :], 1.0 / D, EPS, ALU.mult, ALU.add).then_inc(ms_done, 1)
                    eng.wait_ge(rms_done, t + 1)
                    ch.link(eng.reciprocal(rstd[:, sl, :], rms[:, sl, :]))
                    wait_if(eng, hT_made, t)
                    eng.scalar_tensor_tensor(out=permuted(h[:]), in0=natural(x[:, sl, :]), scalar=rstd[:, sl, :],
                                             in1=natural(gain[:]), op0=ALU.mult, op1=ALU.mult).then_inc(h_done, 1)

                ch.base = 4
                norm(0, 0)

                def q_out(t, n):
                    eng.wait_ge(qkv_made, 3 * t + n + 1)
                    eng.scalar_tensor_tensor(out=q[:, 512 * n:512 * n + 512], in0=ps_q[:, n, :], scalar=HD ** -0.5,
                                             in1=bias[:, 512 * n:512 * n + 512], op0=ALU.mult, op1=ALU.add).then_inc(qkv_done, 1)

                q_out(0, 0)
                q_out(0, 1)

                def body(t, sl, last):
                    ch.base, ch.n = 5 + t * STEPS, 0
                    eng.wait_ge(qkv_made, 3 * t + 3)
                    eng.tensor_tensor(kv[:, sl, :], ps_q[:, 0, :], bias[:, D:QKV], ALU.add).then_inc(qkv_done, 1)
                    if last:
                        return
                    norm(t + 1, 1 - sl)

                    def evacuate(half):
                        a = 8 * half
                        eng.wait_ge(es_done, 2 * t + half + 1)
                        eng.wait_ge(p_done, 16 * t + 8 * half + 8)
                        ch.link(eng.tensor_tensor(tmp[:, a:a + 8], den[:, a:a + 8], esink[:, a:a + 8], ALU.add))
                        ch.link(eng.reciprocal(tmp[:, a:a + 8], tmp[:, a:a + 8]))
                        eng.wait_ge(o_made, PAIRS * t + 4 * half + 4)
                        eng.tensor_tensor(o_all[:, t, 512 * half:512 * half + 512].rearrange("p (h d) -> p h d", h=8), ps_o[:],
                                          tmp[:, a:a + 8].unsqueeze(2).to_broadcast([P, 8, HD]), ALU.mult).then_inc(o_done, 1)

                    for i in range(PAIRS):
                        n = PAIRS * t + i
                        u = i % 2
                        eng.wait_ge(s_made, n + 1)
                        wait_if(eng, p_done, 2 * n - 2)
                        for j in range(2):
                            ch_ins = eng.scalar_tensor_tensor(
                                out=s[:, u, j, :], in0=dist[:, 0 if isinstance(t, int) and t == 0 else 1, :],
                                scalar=SLOPES[head(i, j)], in1=ps_s[:, u, j, :], op0=ALU.mult, op1=ALU.add)
                            ch_ins.then_inc(chain, 1)
                            ch.n += 1
                        eng.wait_ge(chain, ch.base + ch.n)
                        both = slice(head(i, 0), head(i, 1) + 1, 2)
                        ch.link(eng.tensor_reduce(nm[:, both], s[:, u], AX.X, ALU.max, negate=True))
                        ch.link(eng.tensor_tensor(nm[:, both], nm[:, both], nsink[:, both], ALU.min))
                        eng.sem_inc(s_done, 1)
                        if i % 4 == 3:
                            a = 2 * i - 6
                            ch.link(eng.tensor_tensor(tmp[:, a:a + 8], nm[:, a:a + 8], sink[:, a:a + 8], ALU.add))
                            eng.sem_inc(es_in, 1)
                        if i == 5:
                            evacuate(0)
                    q_out(t + 1, 0)
                    evacuate(1)
                    q_out(t + 1, 1)
                    assert ch.n == STEPS
                over_tiles(eng, body)

            @block.tensor
            def _(eng):
                def h_turn(t):
                    eng.wait_ge(h_done, t + 1)
                    wait_if(eng, qkT_done, 2 * t - 1)
                    for k in range(KC):
                        ins = eng.transpose(ps_t[:, P * k:P * k + P], h[:, P * k:P * k + P], ident[:])
                    ins.then_inc(hT_made, 1)

                def project(n, k):
                    ins = eng.matmul(ps_q[:, n % 2, :], hT[:, k, :], w[:, k, 512 * n:512 * n + 512], start=k == 0, stop=k == KC - 1)
                    if k == KC - 1:
                        ins.then_inc(qkv_made, 1)

                h_turn(0)
                eng.wait_ge(hT_done, 1)
                for n in range(2):
                    eng.wait_ge(w_in[n], 16 * (KC // 2))
                    for k in range(KC):
                        project(n, k)

                def body(t, sl, last):
                    if isinstance(t, int) and t == 0:
                        eng.wait_ge(w_in[2], 16 * (KC // 2))
                    eng.wait_ge(qkv_done, 3 * t + 1)
                    for k in range(KC):
                        project(2, k)
                    if last:
                        return
                    eng.wait_ge(qkv_done, 3 * t + 2)
                    for k in range(KC):
                        ins = eng.transpose(ps_t[:, P * k:P * k + P], q[:, P * k:P * k + P], ident[:])
                    ins.then_inc(qkT_made, 1)
                    eng.wait_ge(kdup_done, 2 * t + 2)
                    wait_if(eng, pT_done, PAIRS * t)
                    for g in range(KVH):
                        ins = eng.transpose(ps_p[:, g, :], kdup[:, g].rearrange("p a d -> p (a d)"), ident[:])
                    ins.then_inc(qkT_made, 1)

                    def scores(i):
                        wait_if(eng, s_done, PAIRS * t + i - 1)
                        g = i // 2
                        a = HD * (i % 2)
                        for j in range(2):
                            for b, which in enumerate((1 - sl, sl)):
                                ins = eng.matmul(ps_s[:, i % 2, j, WIN * b:WIN * b + WIN], qT[a:a + HD, 2 * g + j, :],
                                                 kT[a:a + HD, which, g, :], start=True, stop=True)
                        ins.then_inc(s_made, 1)

                    def turn(i):
                        n = PAIRS * t + i
                        eng.wait_ge(p_done, 2 * n + 2)
                        wait_if(eng, pT_done, n)
                        for j in range(2):
                            for b in range(2):
                                ins = eng.transpose(ps_p[:, 2 * j + b, :], p[:, i % 2, j, WIN * b:WIN * b + WIN], ident[:])
                        ins.then_inc(pT_made, 1)

                    def values(i):
                        n = PAIRS * t + i
                        eng.wait_ge(pT_done, n + 1)
                        if i % 4 == 0:
                            wait_if(eng, o_done, 2 * t + i // 4)
                        g = i // 2
                        for j in range(2):
                            for b, which in enumerate((1 - sl, sl)):
                                ins = eng.matmul(ps_o[:, head(i, j) % 8, :], pT[:, i % 2, 2 * j + b, :],
                                                 kv[:, which, KVW + HD * g:KVW + HD * g + HD], start=b == 0, stop=b == 1)
                        ins.then_inc(o_made, 1)

                    eng.wait_ge(qkT_done, 2 * t + 2)
                    step = 0
                    for i in range(PAIRS + 2):
                        if i < PAIRS:
                            scores(i)
                        if i == 1:
                            h_turn(t + 1)
                            eng.wait_ge(hT_done, t + 2)
                            eng.wait_ge(qkv_done, 3 * t + 3)
                        for _ in range((0, 3, 3, 2, 2, 2, 2, 2, 0, 0)[i]):
                            project(step // KC, step % KC)
                            step += 1
                        if 1 <= i <= PAIRS:
                            turn(i - 1)
                        if i >= 2:
                            values(i - 2)
                over_tiles(eng, body)
        swa_sample_attention(nc, io, dram, cst, o_all, stack, q, kv, sink, ps_t, ps_q, ps_s, ps_p, ps_o)


def swa_sample_attention(nc, io, dram, cst, o_all, stack, q, kv, sink, ps_t, ps_q, ps_s, ps_p, ps_o):
    ident = cst["ident"]
    NK = WIN + NT
    with ExitStack() as inner:
        c = Phase(nc, inner, "b_")
        kc = c.sb("kc", [P, NB, KVW])
        vc = c.sb("vc", [P, NB, KVW])
        vn = c.sb("vn", [NT, NB, KVW])
        bias = c.sb("bias", [P, NK])
        sinkr = c.sb("sinkr", [P, 1])
        qs = c.sb("qs", [HD, NB, KVH, 32])
        kT = c.sb("kT", [HD, NB, KVH, NK])
        s = c.sb("s", [P, NB, NK])
        nm, den, es, rden = (c.sb(n, [P, NB]) for n in ("nm", "den", "es", "rden"))
        pT = c.sb("pT", [P, NB, P])
        pnT = c.sb("pnT", [NT, NB, P])
        o = c.sb("o", [P, NB, HD])
        cache_in, vn_in, sink_in, outs, o_out, o_in = (c.sem(n) for n in ("cache_in", "vn_in", "sink_in", "outs", "o_out", "o_in"))
        cleared, turned, copied, q_made, q_done, made, done = (c.sem(n) for n in ("cleared", "turned", "copied", "q_made", "q_done", "made", "done"))
        s_made, s_added, chain, exped = c.sem("s_made"), c.sem("s_added"), c.sem("chain"), c.sem("exped")
        block = inner.enter_context(nc.Block())

        @block.sync
        def _(eng):
            eng.dma_start(kc[:], io["cache_swa_k"][0].rearrange("b w g d -> w b (g d)")).then_inc(cache_in, 16)
            eng.dma_start(vc[:], io["cache_swa_v"][0].rearrange("b w g d -> w b (g d)")).then_inc(cache_in, 16)
            eng.dma_start(bias[:], io["c_swa_sample_bias"]).then_inc(cache_in, 16)
            for b in range(NB):
                eng.dma_start(vn[:, b, :], kv[NT * b:NT * b + NT, 0, KVW:]).then_inc(vn_in, 16)
            for name, src, a in (("k", "cache_swa_k", 0), ("v", "cache_swa_v", KVW)):
                dst = io[f"o_swa_{name}_sample"][0].rearrange("b w g d -> b w (g d)")
                eng.dma_start(dst[:, 0:WIN - NT, :], io[src][0].rearrange("b w g d -> b w (g d)")[:, NT:, :]).then_inc(outs, 16)
                for b in range(NB):
                    eng.dma_start(dst[b, WIN - NT:, :], kv[NT * b:NT * b + NT, 0, a:a + KVW]).then_inc(outs, 16)
            eng.wait_ge(outs, 16 * 2 * (1 + NB))

        @block.scalar
        def _(eng):
            eng.wait_ge(cleared, 1)
            for g in range(KVH):
                for j in range(GRP):
                    r = 32 * g + NT * j
                    src = io["swa_sinks"][0:1, GRP * g + j:GRP * g + j + 1].partition_broadcast(NT)
                    eng.dma_start(sinkr[r:r + NT, :], src).then_inc(sink_in, 16)
            for b in range(0, NB, 2):
                eng.wait_ge(made, b // 2 + 1)
                eng.copy(kT[:, b:b + 2, :, 0:WIN], ps_t[0:HD, :].rearrange("p (b g w) -> p b g w", b=2, g=KVH)).then_inc(done, 1)
            eng.wait_ge(s_added, 1)
            eng.activation(s[:], s[:], ACT.Exp).then_inc(exped, 1)
            eng.activation(es[:], es[:], ACT.Exp).then_inc(exped, 1)
            eng.wait_ge(copied, 1)
            for g in range(KVH):
                for j in range(GRP):
                    r = 32 * g + NT * j
                    eng.dma_start(dram["o_sample"][:, :, GRP * g + j, :].rearrange("b t d -> t b d"), o[r:r + NT]).then_inc(o_out, 16)
            eng.wait_ge(o_out, 16 * HEADS)
            eng.dma_start(o_all[0:NS, PT, :], dram["o_sample"].rearrange("b t h d -> (b t) (h d)")).then_inc(o_in, 16)
            eng.wait_ge(o_in, 16)

        @block.vector
        def _(eng):
            ch = Chain(eng, chain)
            eng.memset(sinkr[:], 0.0).then_inc(cleared, 1)
            eng.memset(o_all[:, PT, :], 0.0).then_inc(chain, 1)
            eng.memset(qs[:], 0.0).then_inc(chain, 1)
            ch.n = 2
            eng.wait_ge(chain, 2)
            eng.wait_ge(q_made, 1)
            for g in range(KVH):
                src = ps_o[0:HD].rearrange("p a (b n) -> p (a b n)", n=32).rearrange("p (g j b t) -> p g j b t", g=KVH, j=GRP, b=NB)
                for j in range(GRP):
                    eng.tensor_copy(qs[:, :, g, NT * j:NT * j + NT], src[:, g, j]).then_inc(q_done, 1)
            eng.wait_ge(q_made, 2)
            src = ps_p[0:HD, 0, :].rearrange("p (g b t) -> p g b t", g=KVH, b=NB)
            for g in range(KVH):
                eng.tensor_copy(kT[:, :, g, WIN:], src[:, g]).then_inc(q_done, 1)
            eng.wait_ge(cache_in, 48)
            for n, bank in enumerate((ps_s[:, 0], ps_s[:, 1], ps_q[:, 0, :])):
                nb = min(3, NB - 3 * n)
                flat = bank.rearrange("p a b -> p (a b)") if n < 2 else bank
                eng.wait_ge(s_made, n + 1)
                eng.tensor_tensor(s[:, 3 * n:3 * n + nb, :], flat[:, 0:nb * NK].rearrange("p (b k) -> p b k", b=nb),
                                  bias[:].unsqueeze(1).to_broadcast([P, nb, NK]), ALU.add).then_inc(chain, 1)
                ch.n += 1
            eng.wait_ge(chain, ch.n)
            ch.link(eng.tensor_reduce(nm[:], s[:], AX.X, ALU.max, negate=True))
            eng.wait_ge(sink_in, 16 * HEADS)
            ch.link(eng.tensor_scalar(es[:], nm[:], sinkr[:], None, ALU.add))
            ch.link(eng.tensor_scalar(es[:], es[:], 0.0, None, ALU.min))
            ch.link(eng.tensor_scalar(nm[:], es[:], sinkr[:], None, ALU.subtract))
            ch.link(eng.tensor_tensor(s[:], s[:], nm[:].unsqueeze(2).to_broadcast([P, NB, NK]), ALU.add))
            eng.sem_inc(s_added, 1)
            eng.wait_ge(exped, 2)
            ch.link(eng.tensor_reduce(den[:], s[:], AX.X, ALU.add))
            ch.link(eng.tensor_tensor(den[:], den[:], es[:], ALU.add))
            ch.link(eng.reciprocal(rden[:], den[:]))
            ch.link(eng.tensor_tensor(s[:], s[:], rden[:].unsqueeze(2).to_broadcast([P, NB, NK]), ALU.mult))
            eng.sem_inc(turned, 1)
            for half in range(2):
                eng.wait_ge(s_made, 4 + half)
                eng.tensor_copy(pT[:, 4 * half:4 * half + 4], ps_p[:]).then_inc(turned, 1)
                eng.tensor_copy(pnT[:, 4 * half:4 * half + 4], ps_q[0:NT, 1, :].rearrange("p (b r) -> p b r", b=4)).then_inc(turned, 1)
            eng.wait_ge(s_made, 6)
            eng.tensor_copy(o[:], ps_o[:]).then_inc(copied, 1)

        @block.tensor
        def _(eng):
            for h in range(HEADS):
                ins = eng.transpose(ps_o[0:HD].rearrange("p a b -> p (a b)")[:, NS * h:NS * h + NS], q[0:NS, HD * h:HD * h + HD], ident[0:NS, 0:NS])
            ins.then_inc(q_made, 1)
            for g in range(KVH):
                ins = eng.transpose(ps_p[0:HD, 0, NS * g:NS * g + NS], kv[0:NS, 0, HD * g:HD * g + HD], ident[0:NS, 0:NS])
            ins.then_inc(q_made, 1)
            eng.wait_ge(cache_in, 48)
            for b in range(0, NB, 2):
                if b:
                    eng.wait_ge(done, b // 2)
                for bb in range(2):
                    for g in range(KVH):
                        a = (bb * KVH + g) * WIN
                        ins = eng.transpose(ps_t[0:HD, a:a + WIN], kc[:, b + bb, HD * g:HD * g + HD], ident[:])
                ins.then_inc(made, 1)
            eng.wait_ge(done, NB // 2)
            eng.wait_ge(q_done, KVH * GRP + KVH)
            for b in range(NB):
                bank = (ps_s[:, 0].rearrange("p a b -> p (a b)"), ps_s[:, 1].rearrange("p a b -> p (a b)"), ps_q[:, 0, :])[b // 3]
                a = (b % 3) * NK
                for g in range(KVH):
                    ins = eng.matmul(bank[32 * g:32 * g + 32, a:a + NK], qs[:, b, g, :], kT[:, b, g, :], start=True, stop=True)
                if b in (2, 5, 7):
                    ins.then_inc(s_made, 1)
            eng.wait_ge(turned, 1)
            for half in range(2):
                if half:
                    eng.wait_ge(turned, 3)
                for b in range(4):
                    eng.transpose(ps_p[:, b, :], s[:, 4 * half + b, 0:WIN], ident[:])
                    ins = eng.transpose(ps_q[0:NT, 1, P * b:P * b + P], s[:, 4 * half + b, WIN:], ident[:])
                ins.then_inc(s_made, 1)
            eng.wait_ge(turned, 5)
            eng.wait_ge(vn_in, 16 * NB)
            for b in range(NB):
                for g in range(KVH):
                    r = slice(32 * g, 32 * g + 32)
                    eng.matmul(ps_o[r, b, :], pT[:, b, r], vc[:, b, HD * g:HD * g + HD], start=True, stop=False)
                    ins = eng.matmul(ps_o[r, b, :], pnT[:, b, r], vn[:, b, HD * g:HD * g + HD], start=False, stop=True)
            ins.then_inc(s_made, 1)


def output_projection_phase(nc, io, dram, cst, layer, o_all, lg):
    ident = cst["ident"]
    w_o, b_o = (io["swa_w_o"], io["swa_b_o"]) if layer == 0 else (io["mla_w_o"], None)
    with ExitStack() as stack:
        c = Phase(nc, stack, f"c{layer}_")
        w = c.sb("w", [P, KC, D])
        wr = c.sb("wr", [P, KC, NG + NE])
        gain = c.sb("gain", [P, D])
        b_out = c.sb("b_out", [P, D])
        b_r = c.sb("b_r", [P, NG + NE])
        x = c.sb("x", [P, 2, D])
        x1 = c.sb("x1", [P, 2, D])
        o = c.sb("o", [P, 2, D])
        junk = c.sb("junk", [P, D])
        ss, ms, rms, rstd = (c.sb(n, [P, 2, 1]) for n in ("ss", "ms", "rms", "rstd"))
        h = c.sb("h", [P, 2, D])
        oT = c.sb("oT", [P, KC, P])
        hT = c.sb("hT", [P, KC, P])
        ps_t = c.ps("ps_t", [P, D])
        ps_y = c.ps("ps_y", [P, 2, 512])
        ps_h = c.ps("ps_h", [P, D])
        ps_r = c.ps("ps_r", [P, 512])
        w_in, small_in = c.sems("w_in", 2), c.sem("small_in")
        x_in, o_in, x1_out, h_out = c.sems("x_in", 2), c.sems("o_in", 2), c.sems("x1_out", 2), c.sems("h_out", 2)
        (oT_made, oT_done, y_made, biased, x1_done, sq_done, ms_done, rms_done, h_done, hT_made, hT_done, r_made, r_done,
         chain) = (c.sem(n) for n in ("oT_made", "oT_done", "y_made", "biased", "x1_done", "sq_done", "ms_done", "rms_done",
                                      "h_done", "hT_made", "hT_done", "r_made", "r_done", "chain"))
        block = stack.enter_context(nc.Block())
        rows = lambda name: dram[name].rearrange("(t p) d -> t p d", p=P)
        prompt = io["x_prompt"][0].rearrange("(t p) d -> t p d", p=P)
        NSMALL = 4 + (layer == 0)

        @block.sync
        def _(eng):
            def body(t, sl, last):
                if isinstance(t, int) and t == 1:
                    for n in range(2):
                        for k in range(0, KC, 2):
                            cols = slice(512 * n, 512 * n + 512)
                            eng.dma_start(w[:, k:k + 2, cols], w_o[0].rearrange("(c p) n -> p c n", p=P)[:, k:k + 2, cols]).then_inc(w_in[n], 16)
                wait_if(eng, oT_made, t - 1)
                eng.dma_start(o[:, sl, :], o_all[:, t, :]).then_inc(o_in[sl], 16)
                wait_if(eng, x1_done, t - 1)
                if layer:
                    src = rows("x_attn")[t]
                else:
                    src = dram["x0"] if last else prompt[t]
                eng.dma_start(x[:, sl, :], src).then_inc(x_in[sl], 16)
            over_tiles(eng, body)

        @block.scalar
        def _(eng):
            eng.dma_start(wr[:, :, 0:NG], io["moe_w_group"][layer].rearrange("(p c) n -> p c n", c=KC)).then_inc(small_in, 16)
            eng.dma_start(wr[:, :, NG:], io["moe_w_expert"][layer].rearrange("(p c) n -> p c n", c=KC)).then_inc(small_in, 16)
            eng.dma_start(gain[:], io["norm_ffn"][layer:layer + 1, :].partition_broadcast(P)).then_inc(small_in, 16)
            eng.dma_start(b_r[:, 0:NG], io["moe_b_group"][layer:layer + 1, :].partition_broadcast(P)).then_inc(small_in, 16)
            eng.dma_start(b_r[:, NG:], io["moe_b_expert"][layer:layer + 1, :].partition_broadcast(P)).then_inc(small_in, 16)
            if layer == 0:
                eng.dma_start(b_out[:], b_o.partition_broadcast(P)).then_inc(small_in, 16)

            def oT_out(t):
                eng.wait_ge(oT_made, t + 1)
                eng.copy(oT[:], ps_t[:].rearrange("p (c j) -> p c j", c=KC)).then_inc(oT_done, 1)

            def hT_out(t):
                eng.wait_ge(hT_made, t + 1)
                eng.copy(hT[:], ps_h[:].rearrange("p (c j) -> p c j", c=KC)).then_inc(hT_done, 1)

            oT_out(0)

            def body(t, sl, last):
                if not isinstance(t, int) or t > 0:
                    hT_out(t - 1)
                if not last:
                    oT_out(t + 1)
                eng.wait_ge(x1_done, t + 1)
                eng.dma_start(rows("x_ffn")[t], x1[:, sl, :]).then_inc(x1_out[sl], 16)
                wait_if(eng, sq_done, t)
                eng.activation(junk[:], x1[:, sl, :], ACT.Square, accum_out=ss[:, sl, :]).then_inc(sq_done, 1)
                eng.wait_ge(ms_done, t + 1)
                eng.activation(rms[:, sl, :], ms[:, sl, :], ACT.Sqrt).then_inc(rms_done, 1)
                eng.wait_ge(h_done, t + 1)
                eng.dma_start(rows("normed")[t], h[:, sl, :]).then_inc(h_out[sl], 16)
            over_tiles(eng, body)
            hT_out(PT)
            for sl in range(2):
                eng.wait_ge(x1_out[sl], nth(PT - sl, sl) if sl == 0 else nth(PT - 1, 1))
                eng.wait_ge(h_out[sl], nth(PT - sl, sl) if sl == 0 else nth(PT - 1, 1))

        @block.gpsimd
        def _(eng):
            if layer == 0:
                eng.wait_ge(small_in, 96)

                def body(t, sl, last):
                    eng.wait_ge(x_in[sl], nth(t, sl))
                    eng.tensor_tensor(x[:, sl, :], x[:, sl, :], b_out[:], ALU.add).then_inc(biased, 1)
                over_tiles(eng, body)

        @block.vector
        def _(eng):
            ch = Chain(eng, chain, 1)
            eng.wait_ge(small_in, 96 if layer == 0 else 80)

            def logits(t):
                eng.wait_ge(r_made, t + 1)
                eng.tensor_tensor(lg[:, t, :], ps_r[:, 0:NG + NE], b_r[:], ALU.add).then_inc(r_done, 1)

            def body(t, sl, last):
                ch.tile(t)
                if layer == 0:
                    eng.wait_ge(biased, t + 1)
                else:
                    eng.wait_ge(x_in[sl], nth(t, sl))
                if not (isinstance(t, int) and t < 2):
                    eng.wait_ge(x1_out[sl], nth(t, sl) - 16)
                    wait_if(eng, sq_done, t - 1)
                eng.wait_ge(y_made, t + 1)
                eng.tensor_tensor(x1[:, sl, :], ps_y[:].rearrange("p a b -> p (a b)"), x[:, sl, :], ALU.add).then_inc(x1_done, 1)
                eng.wait_ge(sq_done, t + 1)
                eng.tensor_scalar(ms[:, sl, :], ss[:, sl, :], 1.0 / D, EPS, ALU.mult, ALU.add).then_inc(ms_done, 1)
                eng.wait_ge(rms_done, t + 1)
                ch.link(eng.reciprocal(rstd[:, sl, :], rms[:, sl, :]))
                if not (isinstance(t, int) and t < 2):
                    eng.wait_ge(h_out[sl], nth(t, sl) - 16)
                    eng.wait_ge(hT_made, t - 1)
                eng.scalar_tensor_tensor(out=permuted(h[:, sl, :]), in0=natural(x1[:, sl, :]), scalar=rstd[:, sl, :],
                                         in1=natural(gain[:]), op0=ALU.mult, op1=ALU.mult).then_inc(h_done, 1)
                if not isinstance(t, int) or t > 0:
                    logits(t - 1)
            over_tiles(eng, body)
            logits(PT)

        @block.tensor
        def _(eng):
            def o_turn(t, sl):
                eng.wait_ge(o_in[sl], nth(t, sl))
                wait_if(eng, oT_done, t)
                for k in range(KC):
                    ins = eng.transpose(ps_t[:, P * k:P * k + P], o[:, sl, P * k:P * k + P], ident[:])
                ins.then_inc(oT_made, 1)

            def h_turn(t, sl):
                eng.wait_ge(h_done, t + 1)
                wait_if(eng, hT_done, t)
                for k in range(KC):
                    ins = eng.transpose(ps_h[:, P * k:P * k + P], h[:, sl, P * k:P * k + P], ident[:])
                ins.then_inc(hT_made, 1)

            def route(t):
                eng.wait_ge(hT_done, t + 1)
                wait_if(eng, r_done, t)
                for k in range(KC):
                    ins = eng.matmul(ps_r[:, 0:NG + NE], hT[:, k, :], wr[:, k, :], start=k == 0, stop=k == KC - 1)
                ins.then_inc(r_made, 1)

            o_turn(0, 0)

            def body(t, sl, last):
                first = isinstance(t, int) and t == 0
                eng.wait_ge(oT_done, t + 1)
                wait_if(eng, x1_done, t)
                for n in range(2):
                    if first:
                        eng.wait_ge(w_in[n], 16 * (KC // 2))
                    for k in range(KC):
                        ins = eng.matmul(ps_y[:, n, :], oT[:, k, :], w[:, k, 512 * n:512 * n + 512], start=k == 0, stop=k == KC - 1)
                    if n == 0 and not first:
                        h_turn(t - 1, 1 - sl)
                ins.then_inc(y_made, 1)
                if not last:
                    o_turn(t + 1, 1 - sl)
                if first:
                    eng.wait_ge(small_in, 96 if layer == 0 else 80)
                else:
                    route(t - 1)
            over_tiles(eng, body)
            h_turn(PT, 0)
            route(PT)


def over_experts(eng, body):
    for e in range(4):
        body(e, e, False)
    with eng.Fori(4, NE - 7, 4) as e:
        for r in range(4):
            body(e + r, r, False)
    for r in range(4):
        body(NE - 4 + r, r, r == 3)


def moe_phase(nc, io, dram, cst, layer, lg, gates):
    ident = cst["ident"]
    with ExitStack() as stack:
        c = Phase(nc, stack, f"m{layer}_")
        w = c.sb("w", [P, 4, 3, KC * DE])
        xg = c.sb("xg", [P, 4, D])
        xT = c.sb("xT", [P, KC, P])
        act = c.sb("act", [P, DE])
        h = c.sb("h", [P, 2, DE])
        hT = c.sb("hT", [P, 2, P])
        y = c.sb("y", [P, 2, D])
        rows_i = c.sb("rows_i", [P, NCOL], I32)
        toks_i = c.sb("toks_i", [P, NCOL], I32)
        row_now = c.sb("row_now", [P, 2], I32)
        tok_now = c.sb("tok_now", [P, 4], I32)
        over_i = c.sb("over_i", [P, MAXOV + 1], I32)
        ps_x = c.ps("ps_x", [P, D])
        ps_gu = c.ps("ps_gu", [P, 2, 2, DE])
        ps_y = c.ps("ps_y", [P, 2, 512])
        ps_h = c.ps("ps_h", [P, 2, P])
        w_in = c.sems("w_in", 4)
        xg_in, y_out = c.sems("xg_in", 4), c.sems("y_out", 2)
        (ix_done, iy_done, xT_made, xT_done, gu_made, act_done, h_done, hT_made, hT_done, y_made, y0_done, y1_done, wiped, passed) = (
            c.sem(n) for n in ("ix_done", "iy_done", "xT_made", "xT_done", "gu_made", "act_done", "h_done", "hT_made", "hT_done",
                               "y_made", "y0_done", "y1_done", "wiped", "passed"))
        T = TILES
        wg = io["moe_w_gate"][layer].rearrange("e (p c) f -> e p (c f)", c=KC)
        wu = io["moe_w_up"][layer].rearrange("e (p c) f -> e p (c f)", c=KC)
        wd = io["moe_w_down"][layer].rearrange("e (p c) n -> e p (c n)", c=2)

        with ExitStack() as inner:
            r = Phase(nc, inner, f"r{layer}_")
            g8 = lambda n: r.sb(n, [P, T, EPG])
            g1 = lambda n: r.sb(n, [P, T])
            eq, sc, ohg, ein, oh1, oh2, ein2, gexp = (g8(n) for n in ("eq", "sc", "ohg", "ein", "oh1", "oh2", "ein2", "gexp"))
            gmax, smax, gate, m1, m2, ed = (g1(n) for n in ("gmax", "smax", "gate", "m1", "m2", "ed"))
            wide = r.sb("wide", [P, T, NE])
            oh = r.sb("oh", [P, 2, T, NE])
            ohs = r.sb("ohs", [P, T + 1, NE])
            pre = r.sb("pre", [P, T + 1, NE])
            cum = r.sb("cum", [P, T, NE])
            cnt = r.sb("cnt", [P, NE])
            pos, blk, col, base, isov = (r.sb(n, [P, 2, T]) for n in ("pos", "blk", "col", "base", "isov"))
            nov = r.sb("nov", [P, NE])
            run = r.sb("run", [P, 2, NE])
            excl = r.sb("excl", [P, NE])
            cmp16 = r.sb("cmp16", [P, MAXOV, NE])
            over = r.sb("over", [P, MAXOV + 1])
            slots = r.sb("slots", [P, 2, T, P])
            cols = r.sb("cols", [P, 2, T, NCOL])
            tbl = r.sb("tbl", [P, NCOL])
            padded = r.sb("padded", [P, NCOL])
            (chain, exp_in, exp_done, oh_in, cum_made, tbl_in, tbl_made) = (
                r.sem(n) for n in ("chain", "exp_in", "exp_done", "oh_in", "cum_made", "tbl_in", "tbl_made"))
            ps_c = ps_gu[:].rearrange("p a b n -> p a (b n)")
            block = inner.enter_context(nc.Block())

            @block.sync
            def _(eng):
                for e in range(4):
                    for n, src in enumerate((wg, wu, wd)):
                        eng.dma_start(w[:, e, n, :], src[e]).then_inc(w_in[e], 16)

            @block.scalar
            def _(eng):
                eng.wait_ge(exp_in, 1)
                eng.activation(gexp[:], gexp[:], ACT.Exp).then_inc(exp_done, 1)
                eng.wait_ge(exp_in, 2)
                eng.activation(ed[:], ed[:], ACT.Exp).then_inc(exp_done, 1)

            @block.tensor
            def _(eng):
                eng.wait_ge(oh_in, 1)
                for n, (a, b) in enumerate(((0, 5), (5, T + 1))):
                    width = (b - a) * NE
                    eng.matmul(ps_c[:, n, 0:width], cst["before"][:], ohs[:, a:b, :], start=True, stop=False)
                    ins = eng.matmul(ps_c[:, n, 0:width], cst["ones"][:], pre[:, a:b, :], start=False, stop=True)
                ins.then_inc(cum_made, 1)
                for k in range(2):
                    for t in range(T):
                        n = k * T + t
                        eng.wait_ge(tbl_in, 2 * n + 2)
                        ins = eng.matmul(ps_h[:].rearrange("p a b -> p (a b)")[:, 0:NCOL], slots[:, k, t, :], cols[:, k, t, :],
                                         start=n == 0, stop=n == 2 * T - 1)
                ins.then_inc(tbl_made, 1)

            @block.vector
            def _(eng):
                ch = Chain(eng, chain)
                link = ch.link
                eng.memset(xg[:], 0.0).then_inc(wiped, 1)
                link(eng.memset(ohs[:, T, :], 0.0))
                link(eng.memset(pre[:, 0, :], 0.0))
                last = lambda a, n: a.unsqueeze(2).to_broadcast([P, T, n])
                rank = cst["rank"][:].unsqueeze(1).to_broadcast([P, T, EPG])

                def first_of_max(src, top, out):
                    link(eng.tensor_reduce(top, src, AX.X, ALU.max))
                    link(eng.tensor_tensor(eq[:], src, last(top, EPG), ALU.is_equal))
                    link(eng.tensor_tensor(sc[:], eq[:], rank, ALU.mult))
                    link(eng.tensor_reduce(smax[:], sc[:], AX.X, ALU.max))
                    link(eng.tensor_tensor(out, sc[:], last(smax[:], EPG), ALU.is_equal))

                g_logits = lg[:, :, 0:NG]
                e_logits = lg[:, :, NG:].rearrange("p t (g e) -> p t g e", g=NG)
                first_of_max(g_logits, gmax[:], ohg[:])
                link(eng.tensor_tensor(gexp[:], g_logits, last(gmax[:], NG), ALU.subtract))
                eng.sem_inc(exp_in, 1)
                wide4 = wide[:].rearrange("p t (g e) -> p t g e", g=NG)
                link(eng.tensor_tensor(wide4, e_logits, ohg[:].unsqueeze(3).to_broadcast([P, T, NG, EPG]), ALU.mult))
                link(eng.tensor_reduce(ein[:], wide[:].rearrange("p t (g e) -> p t e g", g=NG), AX.X, ALU.add))
                first_of_max(ein[:], m1[:], oh1[:])
                link(eng.scalar_tensor_tensor(out=ein2[:], in0=oh1[:], scalar=NEG, in1=ein[:], op0=ALU.mult, op1=ALU.add))
                first_of_max(ein2[:], m2[:], oh2[:])
                link(eng.tensor_tensor(ed[:], m2[:], m1[:], ALU.subtract))
                eng.sem_inc(exp_in, 1)
                link(eng.tensor_tensor(ohg[:], ohg[:], last(cst["valid"][:], NG), ALU.mult))
                for k, o in enumerate((oh1, oh2)):
                    link(eng.tensor_tensor(oh[:, k].rearrange("p t (g e) -> p t g e", g=NG),
                                           ohg[:].unsqueeze(3).to_broadcast([P, T, NG, EPG]),
                                           o[:].unsqueeze(2).to_broadcast([P, T, NG, EPG]), ALU.mult))
                link(eng.tensor_tensor(ohs[:, 0:T, :], oh[:, 0], oh[:, 1], ALU.add))
                for t in range(T):
                    link(eng.tensor_tensor(pre[:, t + 1, :], pre[:, t, :], ohs[:, t, :], ALU.add))
                eng.sem_inc(oh_in, 1)
                eng.wait_ge(exp_done, 2)
                link(eng.tensor_reduce(gate[:], gexp[:], AX.X, ALU.add))
                link(eng.reciprocal(gate[:], gate[:]))
                link(eng.tensor_scalar(m1[:], ed[:], 1.0, None, ALU.add))
                link(eng.reciprocal(m1[:], m1[:]))
                link(eng.tensor_tensor(gates[:, 0, :], m1[:], gate[:], ALU.mult))
                link(eng.tensor_tensor(gates[:, 1, :], gates[:, 0, :], ed[:], ALU.mult))
                eng.wait_ge(cum_made, 1)
                link(eng.tensor_copy(cum[:, 0:5, :], ps_c[:, 0, 0:5 * NE].rearrange("p (t e) -> p t e", e=NE)))
                link(eng.tensor_copy(cum[:, 5:T, :], ps_c[:, 1, 0:(T - 5) * NE].rearrange("p (t e) -> p t e", e=NE)))
                link(eng.tensor_copy(cnt[:], ps_c[:, 1, (T - 5) * NE:(T - 4) * NE]))
                link(eng.tensor_scalar(nov[:], cnt[:], float(P), None, ALU.is_gt))
                for j in range(2, T):
                    link(eng.scalar_tensor_tensor(out=nov[:], in0=cnt[:], scalar=float(P * j), in1=nov[:], op0=ALU.is_gt, op1=ALU.add))
                link(eng.tensor_copy(run[:, 0, :], nov[:]))
                step, at = 1, 0
                while step < NE:
                    link(eng.tensor_copy(run[:, 1 - at, 0:step], run[:, at, 0:step]))
                    link(eng.tensor_tensor(run[:, 1 - at, step:], run[:, at, step:], run[:, at, 0:NE - step], ALU.add))
                    step, at = 2 * step, 1 - at
                incl = run[:, at, :]
                link(eng.tensor_tensor(excl[:], incl, nov[:], ALU.subtract))
                link(eng.tensor_tensor(cmp16[:], incl.unsqueeze(1).to_broadcast([P, MAXOV, NE]),
                                       cst["iota"][:, 0:MAXOV].unsqueeze(2).to_broadcast([P, MAXOV, NE]), ALU.is_le))
                link(eng.tensor_reduce(over[:, 0:MAXOV], cmp16[:], AX.X, ALU.add))
                link(eng.tensor_scalar(over[:, 0:MAXOV], over[:, 0:MAXOV], float(NE - 1), None, ALU.min))
                link(eng.tensor_copy(over[:, MAXOV:], incl[:, NE - 1:NE]))
                link(eng.tensor_copy(over_i[:], over[:]))
                for k in range(2):
                    for out, factor in ((pos, cum[:]), (col, cst["iota"][:, 0:NE].unsqueeze(1).to_broadcast([P, T, NE])),
                                        (base, excl[:].unsqueeze(1).to_broadcast([P, T, NE]))):
                        link(eng.tensor_tensor(wide[:], oh[:, k], factor, ALU.mult))
                        link(eng.tensor_reduce(out[:, k, :], wide[:], AX.X, ALU.add))
                link(eng.tensor_scalar(blk[:], pos[:], float(P), None, ALU.is_ge))
                for j in range(2, T):
                    link(eng.scalar_tensor_tensor(out=blk[:], in0=pos[:], scalar=float(P * j), in1=blk[:], op0=ALU.is_ge, op1=ALU.add))
                link(eng.scalar_tensor_tensor(out=pos[:], in0=blk[:], scalar=-float(P), in1=pos[:], op0=ALU.mult, op1=ALU.add))
                link(eng.tensor_scalar(isov[:], blk[:], 1.0, None, ALU.min))
                link(eng.tensor_tensor(base[:], base[:], blk[:], ALU.add))
                link(eng.tensor_tensor(base[:], base[:], col[:], ALU.subtract))
                link(eng.scalar_tensor_tensor(out=base[:], in0=base[:], scalar=float(NE - 1), in1=isov[:], op0=ALU.add, op1=ALU.mult))
                link(eng.tensor_tensor(col[:], col[:], base[:], ALU.add))
                link(eng.tensor_scalar(m2[:], cst["valid"][:], -1000.0, 1000.0, ALU.mult, ALU.add))
                link(eng.tensor_tensor(col[:], col[:], m2[:].unsqueeze(1).to_broadcast([P, 2, T]), ALU.add))
                link(eng.tensor_copy(base[:, 0, :], cst["aid"][:]))
                link(eng.tensor_scalar(base[:, 1, :], cst["aid"][:], 1.0, None, ALU.add))
                for k in range(2):
                    for t in range(T):
                        eng.tensor_scalar(slots[:, k, t, :], cst["iota"][:], pos[:, k, t:t + 1], None, ALU.is_equal).then_inc(tbl_in, 1)
                        eng.tensor_scalar(cols[:, k, t, :], cst["iota"][:, 0:NCOL], col[:, k, t:t + 1], base[:, k, t:t + 1],
                                          ALU.is_equal, ALU.mult).then_inc(tbl_in, 1)
                eng.wait_ge(tbl_made, 1)
                link(eng.tensor_copy(tbl[:], ps_h[:].rearrange("p a b -> p (a b)")[:, 0:NCOL]))
                link(eng.tensor_scalar(padded[:], tbl[:], 0.0, float(PAD_ROW), ALU.is_equal, ALU.mult))
                link(eng.scalar_tensor_tensor(out=padded[:], in0=tbl[:], scalar=-1.0, in1=padded[:], op0=ALU.add, op1=ALU.add))
                link(eng.tensor_copy(rows_i[:], padded[:]))
                link(eng.tensor_scalar(toks_i[:], rows_i[:], 1, None, ALU.arith_shift_right))

        with ExitStack() as inner:
            block = inner.enter_context(nc.Block())
            stat = lambda k: xT[:, k, :]

            @block.sync
            def _(eng):
                def body(e, slot, last):
                    if isinstance(e, int) and e < 4:
                        return
                    wait_apart(eng, y_made, e - 3, passed)
                    for n, src in enumerate((wg, wu, wd)):
                        eng.dma_start(w[:, slot, n, :], src[e]).then_inc(w_in[slot], 16)
                over_experts(eng, body)

            @block.gpsimd
            def _(eng):
                def gather(e, slot):
                    wait_if(eng, xT_made, e - 3)
                    wait_apart(eng, ix_done, e + 1, passed)
                    eng.indirect_dma_start(out=xg[:, slot, :], out_offset=None, in_=dram["normed"],
                                           in_offset=bass.IndirectOffsetOnAxis(ap=tok_now[:, slot:slot + 1], axis=0),
                                           bounds_check=SEQ + NS - 1, oob_is_err=False).then_inc(xg_in[slot], 16)

                eng.wait_ge(wiped, 1)
                for e in range(3):
                    gather(e, e)

                def body(e, slot, last):
                    u = slot % 2
                    if not (isinstance(e, int) and e >= NE - 3):
                        gather(e + 3, (slot + 3) % 4)
                    eng.wait_ge(y0_done, e + 1)
                    eng.wait_ge(y1_done, e + 1)
                    wait_apart(eng, iy_done, e + 1, passed)
                    eng.indirect_dma_start(out=dram["expert_rows"], out_offset=bass.IndirectOffsetOnAxis(ap=row_now[:, u:u + 1], axis=0),
                                           in_=y[:, u, :], in_offset=None,
                                           bounds_check=2 * (SEQ + NS) - 1, oob_is_err=False).then_inc(y_out[u], 16)
                over_experts(eng, body)
                for u in range(2):
                    eng.wait_ge(y_out[u], 16 * (NE // 2))

            @block.scalar
            def _(eng):
                def xT_out(e):
                    eng.wait_ge(xT_made, e + 1)
                    eng.copy(xT[:], ps_x[:].rearrange("p (c j) -> p c j", c=KC)).then_inc(xT_done, 1)

                def y_copy(e, u):
                    eng.wait_ge(y_made, e + 1)
                    if not (isinstance(e, int) and e < 2):
                        eng.wait_ge(y_out[u], 8 * (e - u))
                    eng.copy(y[:, u, 512:], ps_y[:, 1, :]).then_inc(y1_done, 1)

                xT_out(0)

                def body(e, slot, last):
                    u = slot % 2
                    eng.wait_ge(gu_made, e + 1)
                    wait_if(eng, h_done, e)
                    eng.activation(act[:], ps_gu[:, u, 0, :], ACT.Silu).then_inc(act_done, 1)
                    if not last:
                        xT_out(e + 1)
                    if not (isinstance(e, int) and e == 0):
                        y_copy(e - 1, 1 - u)
                over_experts(eng, body)
                y_copy(NE - 1, 1)

            @block.vector
            def _(eng):
                def index_in(e, slot):
                    if not (isinstance(e, int) and e < 4):
                        eng.wait_ge(xg_in[slot], 4 * (e - slot))
                    eng.tensor_copy(tok_now[:, slot:slot + 1], toks_i[:, bass.ds(e, 1)]).then_inc(ix_done, 1)

                def down_out(e, u):
                    eng.wait_ge(hT_made, e + 1)
                    wait_if(eng, y_made, e)
                    eng.tensor_copy(hT[:], ps_h[:]).then_inc(hT_done, 1)
                    if not (isinstance(e, int) and e < 2):
                        eng.wait_ge(y_out[u], 8 * (e - u))
                    eng.tensor_copy(row_now[:, u:u + 1], rows_i[:, bass.ds(e, 1)]).then_inc(iy_done, 1)
                    eng.wait_ge(y_made, e + 1)
                    eng.tensor_copy(y[:, u, 0:512], ps_y[:, 0, :]).then_inc(y0_done, 1)

                for e in range(3):
                    index_in(e, e)

                def body(e, slot, last):
                    u = slot % 2
                    if not (isinstance(e, int) and e >= NE - 3):
                        index_in(e + 3, (slot + 3) % 4)
                    eng.wait_ge(act_done, e + 1)
                    wait_if(eng, hT_made, e - 1)
                    eng.tensor_tensor(h[:, u].rearrange("p (c j) -> p j c", c=2), act[:].rearrange("p (j c) -> p j c", c=2),
                                      ps_gu[:, u, 1, :].rearrange("p (j c) -> p j c", c=2), ALU.mult).then_inc(h_done, 1)
                    if not (isinstance(e, int) and e == 0):
                        down_out(e - 1, 1 - u)
                over_experts(eng, body)
                down_out(NE - 1, 1)

            @block.tensor
            def _(eng):
                def turn(e, slot):
                    eng.wait_ge(xg_in[slot], 4 * (e - slot) + 16)
                    wait_if(eng, xT_done, e)
                    for k in range(KC):
                        ins = eng.transpose(ps_x[:, P * k:P * k + P], xg[:, slot, P * k:P * k + P], ident[:])
                    ins.then_inc(xT_made, 1)

                def h_turn(e, u):
                    eng.wait_ge(h_done, e + 1)
                    wait_if(eng, hT_done, e)
                    for k in range(2):
                        ins = eng.transpose(ps_h[:, k, :], h[:, u, P * k:P * k + P], ident[:])
                    ins.then_inc(hT_made, 1)

                def down(e, slot):
                    eng.wait_ge(hT_done, e + 1)
                    wait_if(eng, y0_done, e)
                    wait_if(eng, y1_done, e)
                    for n in range(2):
                        for k in range(2):
                            ins = eng.matmul(ps_y[:, n, :], hT[:, k, :], w[:, slot, 2, D * k + 512 * n:D * k + 512 * n + 512],
                                             start=k == 0, stop=k == 1)
                    ins.then_inc(y_made, 1)

                turn(0, 0)

                def body(e, slot, last):
                    u = slot % 2
                    first = isinstance(e, int) and e == 0
                    eng.wait_ge(xT_done, e + 1)
                    eng.wait_ge(w_in[slot], 12 * (e - slot) + 48)
                    wait_if(eng, h_done, e - 1)
                    for k in range(KC):
                        ins = eng.matmul(ps_gu[:, u], xT[:, k, :], w[:, slot, 0:2, DE * k:DE * k + DE], start=k == 0, stop=k == KC - 1)
                        if k == 3 and not first:
                            h_turn(e - 1, 1 - u)
                    ins.then_inc(gu_made, 1)
                    if not last:
                        turn(e + 1, (slot + 1) % 4)
                    if not first:
                        down(e - 1, (slot - 1) % 4)
                over_experts(eng, body)
                h_turn(NE - 1, 1)
                down(NE - 1, 3)

        overflow_blocks(nc, io, dram, cst, layer, w, xg, xT, act, h, hT, y, rows_i, toks_i, row_now, tok_now, over_i,
                        ps_x, ps_gu, ps_y, ps_h, (wg, wu, wd))


def overflow_blocks(nc, io, dram, cst, layer, w, xg, xT, act, h, hT, y, rows_i, toks_i, row_now, tok_now, over_i,
                    ps_x, ps_gu, ps_y, ps_h, weights):
    ident = cst["ident"]
    with ExitStack() as stack:
        c = Phase(nc, stack, f"v{layer}_")
        w_in, x_in, y_out, ix, xT_made, xT_done, gu_made, act_done, h_done, hT_made, hT_done, y_made, y_done, passed = (
            c.sem(n) for n in ("w_in", "x_in", "y_out", "ix", "xT_made", "xT_done", "gu_made", "act_done", "h_done",
                               "hT_made", "hT_done", "y_made", "y_done", "passed"))
        block = stack.enter_context(nc.Block())

        def each(eng, body):
            n = eng.value_load(over_i[0:1, MAXOV:MAXOV + 1], min_val=0, max_val=MAXOV)
            with eng.Fori(0, MAXOV, 1) as j:
                with eng.If(n > j):
                    body(j)

        @block.sync
        def _(eng):
            def body(j):
                e = eng.value_load(over_i[0:1, bass.ds(j, 1)], min_val=0, max_val=NE - 1)
                for n, src in enumerate(weights):
                    eng.dma_start(w[:, 0, n, :], src[e]).then_inc(w_in, 16)
                wait_apart(eng, y_made, j + 1, passed)
            each(eng, body)

        @block.gpsimd
        def _(eng):
            def body(j):
                wait_apart(eng, ix, 2 * j + 2, passed)
                eng.indirect_dma_start(out=xg[:, 0, :], out_offset=None, in_=dram["normed"],
                                       in_offset=bass.IndirectOffsetOnAxis(ap=tok_now[:, 0:1], axis=0),
                                       bounds_check=SEQ + NS - 1, oob_is_err=False).then_inc(x_in, 16)
                wait_apart(eng, y_done, j + 1, passed)
                eng.indirect_dma_start(out=dram["expert_rows"], out_offset=bass.IndirectOffsetOnAxis(ap=row_now[:, 0:1], axis=0),
                                       in_=y[:, 0, :], in_offset=None,
                                       bounds_check=2 * (SEQ + NS) - 1, oob_is_err=False).then_inc(y_out, 16)
                wait_apart(eng, y_out, 16 * j + 16, passed)
            each(eng, body)

        @block.scalar
        def _(eng):
            def body(j):
                eng.wait_ge(xT_made, j + 1)
                eng.copy(xT[:], ps_x[:].rearrange("p (c j) -> p c j", c=KC)).then_inc(xT_done, 1)
                eng.wait_ge(gu_made, j + 1)
                eng.activation(act[:], ps_gu[:, 0, 0, :], ACT.Silu).then_inc(act_done, 1)
            each(eng, body)

        @block.vector
        def _(eng):
            def body(j):
                with_y = 16 * j
                eng.wait_ge(y_out, with_y)
                eng.tensor_copy(tok_now[:, 0:1], toks_i[:, bass.ds(j + NE, 1)]).then_inc(ix, 1)
                eng.tensor_copy(row_now[:, 0:1], rows_i[:, bass.ds(j + NE, 1)]).then_inc(ix, 1)
                eng.wait_ge(act_done, j + 1)
                eng.tensor_tensor(h[:, 0].rearrange("p (c j) -> p j c", c=2), act[:].rearrange("p (j c) -> p j c", c=2),
                                  ps_gu[:, 0, 1, :].rearrange("p (j c) -> p j c", c=2), ALU.mult).then_inc(h_done, 1)
                eng.wait_ge(hT_made, j + 1)
                eng.tensor_copy(hT[:], ps_h[:]).then_inc(hT_done, 1)
                eng.wait_ge(y_made, j + 1)
                eng.tensor_copy(y[:, 0, :], ps_y[:].rearrange("p a b -> p (a b)")).then_inc(y_done, 1)
            each(eng, body)

        @block.tensor
        def _(eng):
            def body(j):
                eng.wait_ge(x_in, 16 * j + 16)
                for k in range(KC):
                    ins = eng.transpose(ps_x[:, P * k:P * k + P], xg[:, 0, P * k:P * k + P], ident[:])
                ins.then_inc(xT_made, 1)
                eng.wait_ge(xT_done, j + 1)
                eng.wait_ge(w_in, 48 * j + 48)
                for k in range(KC):
                    ins = eng.matmul(ps_gu[:, 0], xT[:, k, :], w[:, 0, 0:2, DE * k:DE * k + DE], start=k == 0, stop=k == KC - 1)
                ins.then_inc(gu_made, 1)
                eng.wait_ge(h_done, j + 1)
                for k in range(2):
                    ins = eng.transpose(ps_h[:, k, :], h[:, 0, P * k:P * k + P], ident[:])
                ins.then_inc(hT_made, 1)
                eng.wait_ge(hT_done, j + 1)
                for n in range(2):
                    for k in range(2):
                        ins = eng.matmul(ps_y[:, n, :], hT[:, k, :], w[:, 0, 2, D * k + 512 * n:D * k + 512 * n + 512],
                                         start=k == 0, stop=k == 1)
                ins.then_inc(y_made, 1)
            each(eng, body)


def mla_projection_phase(nc, io, dram, cst, gates, cT, krT, c_sample):
    ident = cst["ident"]
    with ExitStack() as stack:
        c = Phase(nc, stack, "p_")
        w = c.sb("w", [P, KC, DQ])
        wq = c.sb("wq", [P, 3, HEADS * QD])
        gain = c.sb("gain", [P, D])
        gain_q = c.sb("gain_q", [P, QL])
        gain_kv = c.sb("gain_kv", [P, KVL])
        x = c.sb("x", [P, 2, D])
        yr = c.sb("yr", [P, 2, 2, D])
        junk = c.sb("junk", [P, D])
        ss, ms, rms, rstd = (c.sb(n, [P, 3]) for n in ("ss", "ms", "rms", "rstd"))
        h = c.sb("h", [P, D])
        hT = c.sb("hT", [P, KC, P])
        a = c.sb("a", [P, DQ])
        cq = c.sb("cq", [P, QL])
        cqT = c.sb("cqT", [P, 3, P])
        ckv = c.sb("ckv", [P, 2, KVL])
        kr = c.sb("kr", [P, 2, ROPE])
        t4 = c.sb("t4", [P, 4, HEADS, ROPE // 2])
        q = c.sb("q", [P, HEADS, QD])
        qT = c.sb("qT", [QD, HEADS, P])
        ps_t = c.ps("ps_t", [P, D])
        ps_q = c.ps("ps_q", [P, 3, 512])
        ps_c = c.ps("ps_c", [P, 512])
        ps_k = c.ps("ps_k", [P, 512])
        w_in, wq_in, small_in = c.sem("w_in"), c.sem("wq_in"), c.sem("small_in")
        x_in, c_out = c.sems("x_in", 2), c.sems("c_out", 2)
        x2_out, qT_out = c.sems("x2_out", 2), c.sem("qT_out")
        (x2_done, sq_done, ms_done, rms_done, h_done, hT_made, hT_done, a_made, a_done, sq2_done, ms2_done, rms2_done, c_done,
         cT_made, cT_done, q_made, q_done, qr_done, qT_made, qT_done, chain) = (c.sem(n) for n in (
             "x2_done", "sq_done", "ms_done", "rms_done", "h_done", "hT_made", "hT_done", "a_made", "a_done", "sq2_done", "ms2_done",
             "rms2_done", "c_done", "cT_made", "cT_done", "q_made", "q_done", "qr_done", "qT_made", "qT_done", "chain"))
        rows = lambda name: dram[name].rearrange("(t p) d -> t p d", p=P)
        block = stack.enter_context(nc.Block())

        @block.sync
        def _(eng):
            ys = dram["expert_rows"].rearrange("(t p k) d -> t p k d", p=P, k=2)

            def load(t, sl):
                eng.dma_start(x[:, sl, :], rows("x_ffn")[t]).then_inc(x_in[sl], 16)
                eng.dma_start(yr[:, sl], ys[t]).then_inc(x_in[sl], 16)
            load(0, 0)
            for k in range(KC):
                eng.dma_start(w[:, k, :], io["mla_w_dqkv"][0].rearrange("(p c) n -> p c n", c=KC)[:, k, :]).then_inc(w_in, 16)
            load(1, 1)
            for k in range(3):
                eng.dma_start(wq[:, k, :], io["mla_w_uq"][0].rearrange("(c p) n -> p c n", p=P)[:, k, :]).then_inc(wq_in, 16)

            def body(t, sl, last):
                if isinstance(t, int) and t < 2:
                    return
                eng.wait_ge(h_done, t - 1)
                eng.wait_ge(x2_out[sl], nth(t, sl) - 16)
                load(t, sl)
            over_tiles(eng, body)

        @block.gpsimd
        def _(eng):
            lat = io["o_mla_latent_prompt"][0, 0].rearrange("(t p) d -> t p d", p=P)
            rot = io["o_mla_krope_prompt"][0, 0].rearrange("(t p) d -> t p d", p=P)

            def body(t, sl, last):
                eng.wait_ge(c_done, t + 1)
                if last:
                    eng.dma_start(io["o_mla_latent_sample"][0].rearrange("b t d -> (b t) d"), ckv[0:NS, sl, :]).then_inc(c_out[sl], 16)
                    eng.dma_start(io["o_mla_krope_sample"][0].rearrange("b t d -> (b t) d"), kr[0:NS, sl, :]).then_inc(c_out[sl], 16)
                else:
                    eng.dma_start(lat[t], ckv[:, sl, :]).then_inc(c_out[sl], 16)
                    eng.dma_start(rot[t], kr[:, sl, :]).then_inc(c_out[sl], 16)
            over_tiles(eng, body)
            eng.wait_ge(c_out[0], 32 * 5)
            eng.wait_ge(c_out[1], 32 * 4)

        @block.scalar
        def _(eng):
            eng.dma_start(gain[:], io["norm_attn"][1:2, :].partition_broadcast(P)).then_inc(small_in, 16)
            eng.dma_start(gain_q[:], io["mla_norm_q"].partition_broadcast(P)).then_inc(small_in, 16)
            eng.dma_start(gain_kv[:], io["mla_norm_kv"].partition_broadcast(P)).then_inc(small_in, 16)
            qh = dram["q_heads"].rearrange("h d (t p) -> t d h p", p=P)

            def norm(t, sl):
                eng.wait_ge(x2_done, t + 1)
                eng.dma_start(rows("x_attn")[t], x[:, sl, :]).then_inc(x2_out[sl], 16)
                wait_if(eng, sq2_done, 2 * t)
                eng.activation(junk[:], x[:, sl, :], ACT.Square, accum_out=ss[:, 0:1]).then_inc(sq_done, 1)
                eng.wait_ge(ms_done, t + 1)
                eng.activation(rms[:, 0:1], ms[:, 0:1], ACT.Sqrt).then_inc(rms_done, 1)

            def hT_out(t):
                eng.wait_ge(hT_made, t + 1)
                eng.copy(hT[:], ps_t[:].rearrange("p (c j) -> p c j", c=KC)).then_inc(hT_done, 1)

            def q_out(t):
                eng.wait_ge(q_made, t + 1)
                wait_if(eng, qT_made, 2 * t)
                eng.copy(q[:].rearrange("p h d -> p (h d)"), ps_q[:].rearrange("p a b -> p (a b)")).then_inc(q_done, 1)

            def qT_copy(t):
                wait_if(eng, qT_out, 16 * t)
                for half in range(2):
                    eng.wait_ge(qT_made, 2 * t + half + 1)
                    eng.copy(qT[:, 8 * half:8 * half + 8, :], ps_t[0:QD, :].rearrange("p (h j) -> p h j", h=8)).then_inc(qT_done, 1)
                eng.wait_ge(qT_done, 2 * t + 2)
                eng.dma_start(qh[t], qT[:]).then_inc(qT_out, 16)

            norm(0, 0)
            hT_out(0)

            def body(t, sl, last):
                eng.wait_ge(a_made, t + 1)
                wait_if(eng, c_done, t)
                eng.copy(a[:, 0:512], ps_q[:, 0, :]).then_inc(a_done, 1)
                eng.copy(a[:, 512:DQ], ps_q[:, 1, 0:DQ - 512]).then_inc(a_done, 1)
                eng.wait_ge(a_done, 2 * t + 2)
                eng.wait_ge(sq_done, t + 1)
                eng.activation(junk[:, 0:QL], a[:, 0:QL], ACT.Square, accum_out=ss[:, 1:2]).then_inc(sq2_done, 1)
                eng.wait_ge(sq2_done, 2 * t + 1)
                eng.activation(junk[:, 0:KVL], a[:, QL:QL + KVL], ACT.Square, accum_out=ss[:, 2:3]).then_inc(sq2_done, 1)
                eng.wait_ge(ms2_done, t + 1)
                eng.activation(rms[:, 1:3], ms[:, 1:3], ACT.Sqrt).then_inc(rms2_done, 1)
                if not last:
                    norm(t + 1, 1 - sl)
                if not isinstance(t, int) or t > 0:
                    q_out(t - 1)
                if not last:
                    hT_out(t + 1)
                eng.wait_ge(cT_made, t + 1)
                eng.copy(cqT[:], ps_c[:, 0:QL].rearrange("p (c j) -> p c j", c=3)).then_inc(cT_done, 1)
                eng.copy(krT[NOPE:QD, bass.ds(t * P, P)], ps_c[0:ROPE, QL:QL + P]).then_inc(cT_done, 1)
                for k in range(2):
                    eng.copy(cT[:, k, bass.ds(t * P, P)], ps_k[:, P * k:P * k + P]).then_inc(cT_done, 1)
                if not isinstance(t, int) or t > 0:
                    qT_copy(t - 1)
            over_tiles(eng, body)
            q_out(PT)
            qT_copy(PT)
            eng.wait_ge(qT_out, 16 * TILES)
            eng.wait_ge(x2_out[0], 16 * 5)
            eng.wait_ge(x2_out[1], 16 * 4)

        @block.vector
        def _(eng):
            NORM, LATE, ROT = 2, 4 + 6, 6
            ch = Chain(eng, chain)
            eng.wait_ge(small_in, 48)

            def norm(t, sl):
                eng.wait_ge(x_in[sl], 2 * nth(t, sl))
                ch.link(eng.scalar_tensor_tensor(out=x[:, sl, :], in0=yr[:, sl, 0, :], scalar=gates[:, 0, bass.ds(t, 1)], in1=x[:, sl, :],
                                                 op0=ALU.mult, op1=ALU.add))
                eng.scalar_tensor_tensor(out=x[:, sl, :], in0=yr[:, sl, 1, :], scalar=gates[:, 1, bass.ds(t, 1)], in1=x[:, sl, :],
                                         op0=ALU.mult, op1=ALU.add).then_inc(x2_done, 1)
                eng.wait_ge(sq_done, t + 1)
                eng.tensor_scalar(ms[:, 0:1], ss[:, 0:1], 1.0 / D, EPS, ALU.mult, ALU.add).then_inc(ms_done, 1)
                eng.wait_ge(rms_done, t + 1)
                ch.link(eng.reciprocal(rstd[:, 0:1], rms[:, 0:1]))
                wait_if(eng, hT_made, t)
                eng.scalar_tensor_tensor(out=permuted(h[:]), in0=natural(x[:, sl, :]), scalar=rstd[:, 0:1],
                                         in1=natural(gain[:]), op0=ALU.mult, op1=ALU.mult).then_inc(h_done, 1)

            def rotate(t, src, dst, heads, out_sem):
                cos, sin = (cst["rope"][:, bass.ds(t, 1), n, :].to_broadcast([P, heads, ROPE // 2]) for n in range(2))
                lo, hi = src[:, :, 0:16], src[:, :, 16:32]
                for n, (part, f) in enumerate(((lo, cos), (hi, sin), (hi, cos), (lo, sin))):
                    eng.tensor_tensor(t4[:, n, 0:heads, :], part, f, ALU.mult).then_inc(chain, 1)
                    ch.n += 1
                eng.wait_ge(chain, ch.base + ch.n)
                ch.link(eng.tensor_tensor(dst[:, :, 0:16], t4[:, 0, 0:heads, :], t4[:, 1, 0:heads, :], ALU.subtract))
                ch.link(eng.tensor_tensor(dst[:, :, 16:32], t4[:, 2, 0:heads, :], t4[:, 3, 0:heads, :], ALU.add))
                eng.sem_inc(out_sem, 1)

            def rotate_q(t):
                eng.wait_ge(q_done, t + 1)
                v = q[:, :, NOPE:QD]
                rotate(t, v, v, HEADS, qr_done)

            PER = LATE + NORM + ROT
            norm(0, 0)

            def body(t, sl, last):
                ch.base, ch.n = NORM + (t * PER - (0 if isinstance(t, int) and t == 0 else ROT)), 0
                eng.wait_ge(sq2_done, 2 * t + 2)
                ch.link(eng.tensor_scalar(ms[:, 1:2], ss[:, 1:2], 1.0 / QL, EPS, ALU.mult, ALU.add))
                eng.tensor_scalar(ms[:, 2:3], ss[:, 2:3], 1.0 / KVL, EPS, ALU.mult, ALU.add).then_inc(ms2_done, 1)
                eng.wait_ge(rms2_done, t + 1)
                ch.link(eng.reciprocal(rstd[:, 1:3], rms[:, 1:3]))
                if not (isinstance(t, int) and t < 2):
                    eng.wait_ge(c_out[sl], 2 * nth(t, sl) - 32)
                wait_if(eng, cT_made, t)
                eng.scalar_tensor_tensor(out=cq[:], in0=a[:, 0:QL], scalar=rstd[:, 1:2], in1=gain_q[:], op0=ALU.mult,
                                         op1=ALU.mult).then_inc(chain, 1)
                eng.scalar_tensor_tensor(out=ckv[:, sl, :], in0=a[:, QL:QL + KVL], scalar=rstd[:, 2:3], in1=gain_kv[:],
                                         op0=ALU.mult, op1=ALU.mult).then_inc(chain, 1)
                ch.n += 2
                rotate(t, a[:, QL + KVL:].unsqueeze(1), kr[:, sl, :].unsqueeze(1), 1, c_done)
                if not last:
                    norm(t + 1, 1 - sl)
                if not isinstance(t, int) or t > 0:
                    rotate_q(t - 1)
            over_tiles(eng, body)
            rotate_q(PT)
            eng.tensor_copy(c_sample[:], ckv[0:NS, 0, :])

        @block.tensor
        def _(eng):
            def h_turn(t):
                eng.wait_ge(h_done, t + 1)
                wait_if(eng, qT_done, 2 * t - 4)
                for k in range(KC):
                    ins = eng.transpose(ps_t[:, P * k:P * k + P], h[:, P * k:P * k + P], ident[:])
                ins.then_inc(hT_made, 1)

            def queries(t):
                eng.wait_ge(a_done, 2 * t + 4 if not (isinstance(t, int) and t == PT) else 2 * t + 2)
                eng.wait_ge(cT_done, 4 * t + 4)
                for n in range(3):
                    for k in range(3):
                        ins = eng.matmul(ps_q[:, n, :], cqT[:, k, :], wq[:, k, 512 * n:512 * n + 512], start=k == 0, stop=k == 2)
                ins.then_inc(q_made, 1)

            def q_turn(t):
                eng.wait_ge(qr_done, t + 1)
                wait_if(eng, qT_done, 2 * t)
                for half in range(2):
                    if half:
                        eng.wait_ge(qT_done, 2 * t + 1)
                    for i in range(8):
                        ins = eng.transpose(ps_t[0:QD, P * i:P * i + P], q[:, 8 * half + i, :], ident[:])
                    ins.then_inc(qT_made, 1)

            h_turn(0)
            eng.wait_ge(w_in, 16 * KC)

            def body(t, sl, last):
                eng.wait_ge(hT_done, t + 1)
                wait_if(eng, q_done, t - 1)
                for n, width in enumerate((512, DQ - 512)):
                    for k in range(KC):
                        ins = eng.matmul(ps_q[:, n, 0:width], hT[:, k, :], w[:, k, 512 * n:512 * n + width],
                                         start=k == 0, stop=k == KC - 1)
                ins.then_inc(a_made, 1)
                if isinstance(t, int) and t == 1:
                    eng.wait_ge(wq_in, 16 * 3)
                if not isinstance(t, int) or t > 0:
                    queries(t - 1)
                if not last:
                    h_turn(t + 1)
                eng.wait_ge(c_done, t + 1)
                wait_if(eng, cT_done, 4 * t)
                for k in range(3):
                    eng.transpose(ps_c[:, P * k:P * k + P], cq[:, P * k:P * k + P], ident[:])
                eng.transpose(ps_c[0:ROPE, QL:QL + P], kr[:, sl, :], ident[:])
                for k in range(2):
                    ins = eng.transpose(ps_k[:, P * k:P * k + P], ckv[:, sl, P * k:P * k + P], ident[:])
                ins.then_inc(cT_made, 1)
                if not isinstance(t, int) or t > 0:
                    if not last:
                        eng.wait_ge(hT_done, t + 2)
                    q_turn(t - 1)
            over_tiles(eng, body)
            queries(PT)
            q_turn(PT)


def mla_prompt_phase(nc, io, dram, cst, cT, krT, o_all, w_uv):
    ORDER = list(range(PT - 1, -1, -1))
    ident = cst["ident"]
    SC = float(QD) ** -0.5
    with ExitStack() as stack:
        c = Phase(nc, stack, "h_")
        v = c.sb("v", [P, PT, HEADS * HD])
        qT = c.sb("qT", [QD, 2, SEQ])
        kT = c.sb("kT", [QD, 2, SEQ])
        wk = c.sb("wk", [P, 2, 2, NOPE])
        p = c.sb("p", [P, 2, SEQ])
        pT = c.sb("pT", [P, 2, PT, P])
        nm = c.sb("nm", [P, 2, PT])
        den = c.sb("den", [P, PT])
        rden = c.sb("rden", [P, PT])
        ps_s = c.ps("ps_s", [P, 2, SEQ])
        ps_p = c.ps("ps_p", [P, SEQ])
        ps_o = c.ps("ps_o", [P, PT, HD])
        wv_in, rot_in = c.sem("wv_in"), c.sem("rot_in")
        q_in = c.sems("q_in", 2)
        (v_made, v_done, kn_made, kn_done, s_made, masked, nm_done, p_done, pT_made, pT_done, o_made, o_done, den_used, chain) = (
            c.sem(n) for n in ("v_made", "v_done", "kn_made", "kn_done", "s_made", "masked", "nm_done", "p_done", "pT_made",
                               "pT_done", "o_made", "o_done", "den_used", "chain"))
        block = stack.enter_context(nc.Block())

        def over_heads(eng, body):
            body(0, 0, False)
            body(1, 1, False)
            with eng.Fori(2, HEADS - 3, 2) as hh:
                body(hh, 0, False)
                body(hh + 1, 1, False)
            body(HEADS - 2, 0, False)
            body(HEADS - 1, 1, True)

        @block.sync
        def _(eng):
            eng.dma_start(w_uv[:], io["mla_w_uv"][0].rearrange("(c p) h d -> p c (h d)", p=P)).then_inc(wv_in, 16)
            for sl in range(2):
                eng.dma_start(kT[NOPE:QD, sl, :], krT[NOPE:QD, 0:SEQ]).then_inc(rot_in, 16)

            def body(hh, sl, last):
                if not (isinstance(hh, int) and hh < 2):
                    eng.wait_ge(o_made, hh - 1)
                eng.dma_start(qT[:, sl, :], dram["q_heads"][hh][:, 0:SEQ]).then_inc(q_in[sl], 16)
                eng.dma_start(wk[:, sl], io["mla_w_uk"][0].rearrange("(c p) h d -> h p c d", p=P)[hh]).then_inc(q_in[sl], 16)
            over_heads(eng, body)

        @block.scalar
        def _(eng):
            for t in range(PT):
                eng.wait_ge(v_made, t + 1)
                eng.copy(v[:, t, :], ps_s[:, t % 2, :]).then_inc(v_done, 1)

            def keys_out(hh, sl):
                eng.wait_ge(kn_made, hh + 1)
                eng.copy(kT[0:NOPE, sl, :], ps_p[0:NOPE, :]).then_inc(kn_done, 1)

            keys_out(0, 0)

            def body(hh, sl, last):
                for i in range(PT):
                    n = ORDER[i]
                    m = PT * hh + i
                    width = P * (n + 1)
                    eng.wait_ge(nm_done, m + 1)
                    wait_if(eng, pT_made, m - 1)
                    if i == 0:
                        wait_if(eng, den_used, hh)
                    eng.activation(p[:, i % 2, 0:width], ps_s[:, i % 2, 0:width], ACT.Exp, bias=nm[:, 1, n:n + 1], scale=SC,
                                   accum_out=den[:, n:n + 1]).then_inc(p_done, 1)
                    if i == PT // 2 and not last:
                        keys_out(hh + 1, 1 - sl)
                    if n < 4:
                        continue
                    eng.wait_ge(pT_made, m + 1)
                    eng.copy(pT[:, i % 2, 0:n + 1, :], ps_p[:, 0:width].rearrange("p (t j) -> p t j", j=P)).then_inc(pT_done, 1)
            over_heads(eng, body)

        @block.vector
        def _(eng):
            PER = PT + 1
            ch = Chain(eng, chain, PER)

            def rows_out(hh):
                eng.wait_ge(o_made, hh + 1)
                eng.tensor_tensor(o_all[:, 0:PT, bass.ds(hh * HD, HD)], ps_o[:], rden[:].unsqueeze(2).to_broadcast([P, PT, HD]),
                                  ALU.mult).then_inc(o_done, 1)

            def body(hh, sl, last):
                ch.tile(hh)

                def probs_out(i):
                    n = ORDER[i]
                    if n >= 4:
                        return
                    width = P * (n + 1)
                    eng.wait_ge(pT_made, PT * hh + i + 1)
                    eng.tensor_copy(pT[:, i % 2, 0:n + 1, :], ps_p[:, 0:width].rearrange("p (t j) -> p t j", j=P)).then_inc(pT_done, 1)

                for i in range(PT):
                    n = ORDER[i]
                    m = PT * hh + i
                    width = P * (n + 1)
                    eng.wait_ge(s_made, m + 1)
                    eng.tensor_tensor(ps_s[:, i % 2, P * n:width], ps_s[:, i % 2, P * n:width], cst["causal"][:], ALU.add).then_inc(masked, 1)
                    eng.wait_ge(masked, m + 1)
                    if i == 0:
                        wait_if(eng, p_done, m)
                    ch.link(eng.tensor_reduce(nm[:, 0, n:n + 1], ps_s[:, i % 2, 0:width], AX.X, ALU.max, negate=True))
                    eng.tensor_scalar(nm[:, 1, n:n + 1], nm[:, 0, n:n + 1], SC, None, ALU.mult).then_inc(nm_done, 1)
                    if i:
                        probs_out(i - 1)
                    if i == 1 and not (isinstance(hh, int) and hh == 0):
                        rows_out(hh - 1)
                probs_out(PT - 1)
                eng.wait_ge(p_done, PT * hh + PT)
                ch.link(eng.reciprocal(rden[:], den[:]))
                eng.sem_inc(den_used, 1)
            over_heads(eng, body)
            rows_out(HEADS - 1)

        @block.tensor
        def _(eng):
            eng.wait_ge(wv_in, 16)
            for t in range(PT):
                if t >= 2:
                    eng.wait_ge(v_done, t - 1)
                for n in range(2):
                    for k in range(2):
                        ins = eng.matmul(ps_s[:, t % 2, 512 * n:512 * n + 512], cT[:, k, P * t:P * t + P], w_uv[:, k, 512 * n:512 * n + 512],
                                         start=k == 0, stop=k == 1)
                ins.then_inc(v_made, 1)

            def keys(hh, sl):
                eng.wait_ge(q_in[sl], 2 * nth(hh, sl))
                for n in range(2):
                    for k in range(2):
                        ins = eng.matmul(ps_p[0:NOPE, 512 * n:512 * n + 512], wk[:, sl, k, :], cT[:, k, 512 * n:512 * n + 512],
                                         start=k == 0, stop=k == 1)
                ins.then_inc(kn_made, 1)

            keys(0, 0)
            eng.wait_ge(rot_in, 32)
            eng.wait_ge(v_done, PT)

            def scores(hh, sl, i):
                n = ORDER[i]
                m = PT * hh + i
                wait_if(eng, p_done, m - 1)
                for a in range(0, P * (n + 1), 512):
                    b = min(a + 512, P * (n + 1))
                    ins = eng.matmul(ps_s[:, i % 2, a:b], qT[:, sl, P * n:P * n + P], kT[:, sl, a:b], start=True, stop=True)
                ins.then_inc(s_made, 1)

            eng.wait_ge(kn_done, 1)
            scores(0, 0, 0)
            scores(0, 0, 1)

            def body(hh, sl, last):
                def turn(i):
                    n = ORDER[i]
                    m = PT * hh + i
                    eng.wait_ge(p_done, m + 1)
                    wait_if(eng, pT_done, m)
                    for t in range(n + 1):
                        ins = eng.transpose(ps_p[:, P * t:P * t + P], p[:, i % 2, P * t:P * t + P], ident[:])
                    ins.then_inc(pT_made, 1)

                def values(i):
                    n = ORDER[i]
                    eng.wait_ge(pT_done, PT * hh + i + 1)
                    if i == 0:
                        wait_if(eng, o_done, hh)
                    for t in range(n + 1):
                        ins = eng.matmul(ps_o[:, n, :], pT[:, i % 2, t, :], v[:, t, bass.ds(hh * HD, HD)], start=t == 0, stop=t == n)
                    if i == PT - 1:
                        ins.then_inc(o_made, 1)

                for i in range(PT):
                    early = i == PT // 2 and not last
                    if early:
                        eng.wait_ge(pT_done, PT * hh + i)
                        keys(hh + 1, 1 - sl)
                        values(i - 1)
                        eng.wait_ge(kn_done, hh + 2)
                    turn(i)
                    if i + 2 < PT:
                        scores(hh, sl, i + 2)
                    elif not last:
                        scores(hh + 1, 1 - sl, i + 2 - PT)
                    if i and not early:
                        values(i - 1)
                values(PT - 1)
            over_heads(eng, body)


def mla_sample_phase(nc, io, dram, cst, cT, krT, c_sample, o_all, w_uv):
    ident = cst["ident"]
    SC = float(QD) ** -0.5
    R = HEADS * NT
    with ExitStack() as stack:
        c = Phase(nc, stack, "g_")
        table = c.sb("table", [1, NB * PAGES], I32)
        cp = c.sb("cp", [P, 3, PAGES, KVL])
        rp = c.sb("rp", [P, 3, PAGES, ROPE])
        w_uk = c.sb("w_uk", [P, 2, HEADS * NOPE])
        w_ukT = c.sb("w_ukT", [NOPE, HEADS, 2, P])
        qn = c.sb("qn", [NOPE, HEADS, NS])
        qr = c.sb("qr", [ROPE, HEADS, NS])
        qrb = c.sb("qrb", [ROPE, NB, HEADS, NT])
        krn = c.sb("krn", [ROPE, NS])
        qlat = c.sb("qlat", [P, 2, NB, HEADS, NT])
        cn = c.sb("cn", [NT, NB, KVL])
        cpT = c.sb("cpT", [P, 2, 2, SEQ])
        rpT = c.sb("rpT", [ROPE, SEQ])
        causal = c.sb("causal", [R, NT])
        p = c.sb("p", [R, SEQ + NT])
        sn = c.sb("sn", [R, NT])
        nm, den, rden = (c.sb(n, [R, 3]) for n in ("nm", "den", "rden"))
        pT = c.sb("pT", [P, PAGES, R])
        pnT = c.sb("pnT", [NT, R])
        ol = c.sb("ol", [R, KVL])
        olT = c.sb("olT", [P, 2, HEADS, NB, NT])
        ps_a = c.ps("ps_a", [P, D])
        ps_s = c.ps("ps_s", [P, SEQ])
        ps_n = c.ps("ps_n", [P, 512])
        ps_p = c.ps("ps_p", [P, 512])
        ps_o = c.ps("ps_o", [P, 512])
        ps_u = c.ps("ps_u", [P, 512])
        table_in, small_in, page_in = c.sem("table_in"), c.sem("small_in"), c.sems("page_in", 3)
        (wT_made, wT_done, ql_made, ql_done, cT_made, cT_done, s_made, sn_done, p_done, pT_made, pT_done, o_made, o_done, oT_made,
         oT_done, y_made, y_done, chain, den_done) = (c.sem(n) for n in (
             "wT_made", "wT_done", "ql_made", "ql_done", "cT_made", "cT_done", "s_made", "sn_done", "p_done", "pT_made", "pT_done",
             "o_made", "o_done", "oT_made", "oT_done", "y_made", "y_done", "chain", "den_done"))
        block = stack.enter_context(nc.Block())

        @block.sync
        def _(eng):
            eng.dma_start(table[:], io["page_table"].rearrange("b (x n) -> x (b n)", x=1)).then_inc(table_in, 16)
            eng.wait_ge(table_in, 16)
            for b in range(NB):
                if b >= 3:
                    eng.wait_ge(o_made, b - 2)
                for n in range(PAGES):
                    i = b * PAGES + n
                    page = eng.value_load(table[0:1, i:i + 1], min_val=0, max_val=io["cache_mla_latent"].shape[1] - 1)
                    eng.dma_start(cp[:, b % 3, n, :], io["cache_mla_latent"][0][page]).then_inc(page_in[b % 3], 16)
                    eng.dma_start(rp[:, b % 3, n, :], io["cache_mla_krope"][0][page]).then_inc(page_in[b % 3], 16)

        @block.scalar
        def _(eng):
            eng.dma_start(w_uk[:], io["mla_w_uk"][0].rearrange("(c p) h d -> p c (h d)", p=P)).then_inc(small_in, 16)
            eng.dma_start(qn[:], dram["q_heads"][:, 0:NOPE, SEQ:SEQ + NS].rearrange("h d r -> d h r")).then_inc(small_in, 16)
            eng.dma_start(qr[:], dram["q_heads"][:, NOPE:QD, SEQ:SEQ + NS].rearrange("h d r -> d h r")).then_inc(small_in, 16)
            eng.dma_start(causal[:], io["c_sample_causal"]).then_inc(small_in, 16)
            eng.dma_start(krn[:], krT[NOPE:QD, SEQ:SEQ + NS]).then_inc(small_in, 16)
            for b in range(NB):
                eng.dma_start(cn[:, b, :], c_sample[NT * b:NT * b + NT, :]).then_inc(small_in, 16)
            def latents_out(b):
                for k in range(4):
                    eng.wait_ge(cT_made, 5 * b + k + 1)
                    eng.copy(cpT[:, b % 2, :, 256 * k:256 * k + 256],
                             (ps_a[:, 0:512] if k % 2 == 0 else ps_a[:, 512:]).rearrange("p (c j) -> p c j", c=2)).then_inc(cT_done, 1)

            latents_out(0)
            for b in range(NB):
                if b + 1 < NB:
                    latents_out(b + 1)
                eng.wait_ge(sn_done, b + 1)
                if b:
                    eng.wait_ge(pT_made, b)
                    eng.wait_ge(den_done, b)
                eng.activation(p[:, 0:SEQ], ps_s[0:R, :], ACT.Exp, bias=nm[:, 2:3], scale=SC, accum_out=den[:, 0:1]).then_inc(p_done, 1)
                eng.activation(p[:, SEQ:], sn[:], ACT.Exp, bias=nm[:, 2:3], scale=SC, accum_out=den[:, 1:2]).then_inc(p_done, 1)

        @block.vector
        def _(eng):
            ch = Chain(eng, chain)
            ch.link(eng.memset(o_all[:, PT, :], 0.0))
            eng.wait_ge(small_in, 16 * (5 + NB))
            ch.link(eng.tensor_copy(qrb[:].rearrange("p b h t -> p h b t"), qr[:].rearrange("p h (b t) -> p h b t", b=NB)))
            for r in range(4):
                eng.wait_ge(wT_made, r + 1)
                eng.tensor_copy(w_ukT[:, 4 * r:4 * r + 4].rearrange("p h c j -> p (h c j)"), ps_a[0:NOPE, :]).then_inc(wT_done, 1)
            for k in range(2):
                eng.wait_ge(ql_made, 1)
                for b in range(NB):
                    src = ps_s[:, 512 * k:512 * k + 512].rearrange("p (h b t) -> p h b t", h=HEADS, b=NB)[:, :, b, :]
                    ch.link(eng.tensor_copy(qlat[:, k, b], src))
            eng.sem_inc(ql_done, 1)
            for b in range(NB):
                eng.wait_ge(cT_made, 5 * b + 5)
                for half, bank in enumerate((ps_n, ps_u)):
                    eng.tensor_copy(rpT[:, 512 * half:512 * half + 512], bank[0:ROPE, :]).then_inc(cT_done, 1)
                eng.wait_ge(s_made, b + 1)
                ch.link(eng.tensor_tensor(sn[:], ps_n[0:R, 0:NT], causal[:], ALU.add))
                ch.link(eng.tensor_reduce(nm[:, 0:1], ps_s[0:R, :], AX.X, ALU.max, negate=True))
                ch.link(eng.tensor_reduce(nm[:, 1:2], sn[:], AX.X, ALU.max, negate=True))
                ch.link(eng.tensor_tensor(nm[:, 2:3], nm[:, 0:1], nm[:, 1:2], ALU.min))
                ch.link(eng.tensor_scalar(nm[:, 2:3], nm[:, 2:3], SC, None, ALU.mult))
                eng.sem_inc(sn_done, 1)
                eng.wait_ge(p_done, 2 * b + 2)
                ch.link(eng.tensor_tensor(rden[:, 0:1], den[:, 0:1], den[:, 1:2], ALU.add))
                ch.link(eng.reciprocal(rden[:, 1:2], rden[:, 0:1]))
                eng.sem_inc(den_done, 1)
                eng.wait_ge(pT_made, b + 1)
                eng.tensor_copy(pT[:].rearrange("p a r -> p (a r)"), ps_p[:]).then_inc(pT_done, 1)
                eng.tensor_copy(pnT[:], ps_n[0:NT, 0:R]).then_inc(pT_done, 1)
                eng.wait_ge(o_made, b + 1)
                eng.tensor_scalar(ol[:], ps_o[0:R, 0:KVL], rden[:, 1:2], None, ALU.mult).then_inc(o_done, 1)
                eng.wait_ge(oT_made, b + 1)
                for k in range(2):
                    eng.tensor_copy(olT[:, k, :, b, :], ps_u[:, R * k:R * k + R].rearrange("p (h t) -> p h t", h=HEADS)).then_inc(oT_done, 1)
            eng.wait_ge(y_made, 1)
            eng.tensor_copy(o_all[0:NS, PT, :], ps_a[0:NS, :]).then_inc(y_done, 1)

        @block.tensor
        def _(eng):
            eng.wait_ge(small_in, 16 * (5 + NB))
            for r in range(4):
                if r:
                    eng.wait_ge(wT_done, r)
                for i in range(4):
                    for k in range(2):
                        hh = 4 * r + i
                        ins = eng.transpose(ps_a[0:NOPE, (2 * i + k) * P:(2 * i + k + 1) * P], w_uk[:, k, NOPE * hh:NOPE * hh + NOPE], ident[:])
                ins.then_inc(wT_made, 1)
            eng.wait_ge(wT_done, 4)
            for hh in range(HEADS):
                for k in range(2):
                    ins = eng.matmul(ps_s[:, 512 * k + NS * hh:512 * k + NS * hh + NS], w_ukT[:, hh, k, :], qn[:, hh, :], start=True, stop=True)
            ins.then_inc(ql_made, 1)
            eng.wait_ge(ql_done, 1)
            def latents_turn(b):
                sl = b % 3
                eng.wait_ge(page_in[sl], 16 * 2 * PAGES * (b // 3 + 1))
                for k in range(4):
                    if b or k >= 2:
                        eng.wait_ge(cT_done, 6 * b + k - 1 if k >= 2 else 6 * b)
                    bank = ps_a[:, 0:512] if k % 2 == 0 else ps_a[:, 512:]
                    for half in range(2):
                        for n in range(2):
                            ins = eng.transpose(bank[:, 256 * half + P * n:256 * half + P * n + P], cp[:, sl, 2 * k + n, P * half:P * half + P], ident[:])
                    ins.then_inc(cT_made, 1)

            latents_turn(0)
            for b in range(NB):
                sl = b % 3
                if b:
                    eng.wait_ge(pT_done, 2 * b)
                    eng.wait_ge(oT_done, 2 * b)
                for n in range(PAGES):
                    bank = ps_n if n < 4 else ps_u
                    ins = eng.transpose(bank[0:ROPE, P * (n % 4):P * (n % 4) + P], rp[:, sl, n, :], ident[:])
                ins.then_inc(cT_made, 1)
                eng.wait_ge(cT_done, 6 * b + 6)
                lhs = [qlat[:, k, b].rearrange("p h t -> p (h t)") for k in range(2)] + [qrb[:, b].rearrange("p h t -> p (h t)")]
                for half in range(2):
                    cols = slice(512 * half, 512 * half + 512)
                    for k, rhs in enumerate((cpT[:, b % 2, 0, cols], cpT[:, b % 2, 1, cols], rpT[:, cols])):
                        eng.matmul(ps_s[0:R, cols], lhs[k], rhs, start=k == 0, stop=k == 2)
                new = slice(SEQ + NT * b, SEQ + NT * b + NT)
                for k, rhs in enumerate((cT[:, 0, new], cT[:, 1, new], krn[:, NT * b:NT * b + NT])):
                    ins = eng.matmul(ps_n[0:R, 0:NT], lhs[k], rhs, start=k == 0, stop=k == 2)
                ins.then_inc(s_made, 1)
                if b + 1 < NB:
                    latents_turn(b + 1)
                eng.wait_ge(p_done, 2 * b + 2)
                for n in range(PAGES):
                    eng.transpose(ps_p[:, R * n:R * n + R], p[:, P * n:P * n + P], ident[0:R, 0:R])
                ins = eng.transpose(ps_n[0:NT, 0:R], p[:, SEQ:], ident[0:R, 0:R])
                ins.then_inc(pT_made, 1)
                eng.wait_ge(pT_done, 2 * b + 2)
                if b:
                    eng.wait_ge(o_done, b)
                for n in range(PAGES):
                    eng.matmul(ps_o[0:R, 0:KVL], pT[:, n, :], cp[:, sl, n, :], start=n == 0, stop=False)
                ins = eng.matmul(ps_o[0:R, 0:KVL], pnT[:], cn[:, b, :], start=False, stop=True)
                ins.then_inc(o_made, 1)
                eng.wait_ge(o_done, b + 1)
                for k in range(2):
                    ins = eng.transpose(ps_u[:, R * k:R * k + R], ol[:, P * k:P * k + P], ident[0:R, 0:R])
                ins.then_inc(oT_made, 1)
            eng.wait_ge(oT_done, 2 * NB)
            for hh in range(HEADS):
                for k in range(2):
                    ins = eng.matmul(ps_a[0:NS, HD * hh:HD * hh + HD], olT[:, k, hh].rearrange("p b t -> p (b t)"),
                                     w_uv[:, k, HD * hh:HD * hh + HD], start=k == 0, stop=k == 1)
            ins.then_inc(y_made, 1)


def final_phase(nc, io, dram, cst, gates):
    with ExitStack() as stack:
        c = Phase(nc, stack, "f_")
        gain = c.sb("gain", [P, D])
        x = c.sb("x", [P, 2, D])
        yr = c.sb("yr", [P, 2, 2, D])
        out = c.sb("out", [P, 2, D])
        junk = c.sb("junk", [P, D])
        ss, ms, rms, rstd = (c.sb(n, [P, 2, 1]) for n in ("ss", "ms", "rms", "rstd"))
        small_in, chain = c.sem("small_in"), c.sem("chain")
        x_in, stored = c.sems("x_in", 2), c.sems("stored", 2)
        x3_done, sq_done, ms_done, rms_done, y_done = (c.sem(n) for n in ("x3_done", "sq_done", "ms_done", "rms_done", "y_done"))
        block = stack.enter_context(nc.Block())
        rows = dram["x_ffn"].rearrange("(t p) d -> t p d", p=P)
        ys = dram["expert_rows"].rearrange("(t p k) d -> t p k d", p=P, k=2)
        prompt = io["o_y_prompt"][0].rearrange("(t p) d -> t p d", p=P)

        @block.sync
        def _(eng):
            def body(t, sl, last):
                wait_if(eng, y_done, t - 1)
                eng.dma_start(x[:, sl, :], rows[t]).then_inc(x_in[sl], 16)
                eng.dma_start(yr[:, sl], ys[t]).then_inc(x_in[sl], 16)
            over_tiles(eng, body)

        @block.scalar
        def _(eng):
            eng.dma_start(gain[:], io["norm_final"].rearrange("(a d) -> a d", a=1).partition_broadcast(P)).then_inc(small_in, 16)

            def body(t, sl, last):
                eng.wait_ge(x3_done, t + 1)
                wait_if(eng, sq_done, t)
                eng.activation(junk[:], x[:, sl, :], ACT.Square, accum_out=ss[:, sl, :]).then_inc(sq_done, 1)
                eng.wait_ge(ms_done, t + 1)
                eng.activation(rms[:, sl, :], ms[:, sl, :], ACT.Sqrt).then_inc(rms_done, 1)
                eng.wait_ge(y_done, t + 1)
                if last:
                    eng.dma_start(io["o_y_sample"].rearrange("b t d -> (b t) d"), out[0:NS, sl, :]).then_inc(stored[sl], 16)
                else:
                    eng.dma_start(prompt[t], out[:, sl, :]).then_inc(stored[sl], 16)
            over_tiles(eng, body)
            eng.wait_ge(stored[0], 16 * 5)
            eng.wait_ge(stored[1], 16 * 4)

        @block.vector
        def _(eng):
            ch = Chain(eng, chain, 2)
            eng.wait_ge(small_in, 16)

            def body(t, sl, last):
                ch.tile(t)
                eng.wait_ge(x_in[sl], 2 * nth(t, sl))
                ch.link(eng.scalar_tensor_tensor(out=x[:, sl, :], in0=yr[:, sl, 0, :], scalar=gates[:, 0, bass.ds(t, 1)], in1=x[:, sl, :],
                                                 op0=ALU.mult, op1=ALU.add))
                eng.scalar_tensor_tensor(out=x[:, sl, :], in0=yr[:, sl, 1, :], scalar=gates[:, 1, bass.ds(t, 1)], in1=x[:, sl, :],
                                         op0=ALU.mult, op1=ALU.add).then_inc(x3_done, 1)
                eng.wait_ge(sq_done, t + 1)
                eng.tensor_scalar(ms[:, sl, :], ss[:, sl, :], 1.0 / D, EPS, ALU.mult, ALU.add).then_inc(ms_done, 1)
                eng.wait_ge(rms_done, t + 1)
                ch.link(eng.reciprocal(rstd[:, sl, :], rms[:, sl, :]))
                if not (isinstance(t, int) and t < 2):
                    eng.wait_ge(stored[sl], nth(t, sl) - 16)
                eng.scalar_tensor_tensor(out=out[:, sl, :], in0=x[:, sl, :], scalar=rstd[:, sl, :], in1=gain[:],
                                         op0=ALU.mult, op1=ALU.mult).then_inc(y_done, 1)
            over_tiles(eng, body)


OUTPUTS = [
    ("o_y_prompt", (1, SEQ, D)), ("o_y_sample", (NB, NT, D)),
    ("o_swa_k_prompt", (1, 1, WIN, KVH, HD)), ("o_swa_v_prompt", (1, 1, WIN, KVH, HD)),
    ("o_swa_k_sample", (1, NB, WIN, KVH, HD)), ("o_swa_v_sample", (1, NB, WIN, KVH, HD)),
    ("o_mla_latent_prompt", (1, 1, SEQ, KVL)), ("o_mla_krope_prompt", (1, 1, SEQ, ROPE)),
    ("o_mla_latent_sample", (1, NB, NT, KVL)), ("o_mla_krope_sample", (1, NB, NT, ROPE)),
]


def build(nc, io):
    dram = {
        "x0": nc.dram_tensor("x0", (P, D), F32).ap(),
        "x_attn": nc.dram_tensor("x_attn", (ROWS, D), F32).ap(),
        "x_ffn": nc.dram_tensor("x_ffn", (ROWS, D), F32).ap(),
        "normed": nc.dram_tensor("normed", (ROWS, D), F32).ap(),
        "expert_rows": nc.dram_tensor("expert_rows", (2 * ROWS, D), F32).ap(),
        "q_heads": nc.dram_tensor("q_heads", (HEADS, QD, ROWS), F32).ap(),
        "o_sample": nc.dram_tensor("o_sample", (NB, NT, HEADS, HD), F32).ap(),
    }
    with ExitStack() as stack:
        c = Phase(nc, stack, "")
        cst = {
            "ident": c.sb("ident", [P, P]), "before": c.sb("before", [P, P]), "iota": c.sb("iota", [P, P]),
            "ones": c.sb("ones", [P, P]), "causal": c.sb("causal", [P, P]),
            "rope": c.sb("rope", [P, TILES, 2, ROPE // 2]), "valid": c.sb("valid", [P, TILES]),
            "aid": c.sb("aid", [P, TILES]), "rank": c.sb("rank", [P, EPG]),
        }
        lg = c.sb("lg", [P, TILES, NG + NE])
        gates = c.sb("gates", [P, 2, TILES])
        setup_phase(nc, io, dram, cst)
        with ExitStack() as attn:
            o_all = attn.enter_context(nc.sbuf_tensor("o_all0", [P, TILES, D], F32))
            swa_attention_phase(nc, io, dram, cst, o_all)
            output_projection_phase(nc, io, dram, cst, 0, o_all, lg)
        moe_phase(nc, io, dram, cst, 0, lg, gates)
        with ExitStack() as attn:
            o_all = attn.enter_context(nc.sbuf_tensor("o_all1", [P, TILES, D], F32))
            with ExitStack() as lat:
                a = lambda n, sh: lat.enter_context(nc.sbuf_tensor(n, sh, F32))
                cT, krT, c_sample = a("cT", [P, 2, ROWS]), a("krT", [QD, ROWS]), a("c_sample", [NS, KVL])
                w_uv = a("w_uv", [P, 2, HEADS * HD])
                mla_projection_phase(nc, io, dram, cst, gates, cT, krT, c_sample)
                mla_prompt_phase(nc, io, dram, cst, cT, krT, o_all, w_uv)
                mla_sample_phase(nc, io, dram, cst, cT, krT, c_sample, o_all, w_uv)
            output_projection_phase(nc, io, dram, cst, 1, o_all, lg)
        moe_phase(nc, io, dram, cst, 1, lg, gates)
        final_phase(nc, io, dram, cst, gates)


INPUTS = [
    "x_prompt", "x_sample", "cache_swa_k", "cache_swa_v", "cache_mla_latent", "cache_mla_krope", "page_table",
    "norm_attn", "norm_ffn", "norm_final", "swa_w_qkv", "swa_b_qkv", "swa_sinks", "swa_w_o", "swa_b_o",
    "mla_w_dqkv", "mla_norm_q", "mla_norm_kv", "mla_w_uq", "mla_w_uk", "mla_w_uv", "mla_w_o",
    "moe_w_group", "moe_b_group", "moe_w_expert", "moe_b_expert", "moe_w_gate", "moe_w_up", "moe_w_down",
]


def kernel(**inputs):
    import concourse.bacc as bacc
    from concourse.bass_utils import run_bass_kernel_spmd

    nc = bacc.Bacc("TRN2", target_bir_lowering=False, num_devices=1)
    arrays = {name: np.ascontiguousarray(inputs[name]) for name in INPUTS}
    arrays.update(shape_constants())
    io = {}
    for name, a in arrays.items():
        io[name] = nc.dram_tensor(name, a.shape, mybir.dt.from_np(a.dtype), kind="ExternalInput").ap()
    for name, shape in OUTPUTS:
        io[name] = nc.dram_tensor(name, shape, F32, kind="ExternalOutput").ap()
    build(nc, io)
    r = run_bass_kernel_spmd(nc, [arrays], core_ids=[0])
    return tuple(r.results[0][name] for name, _ in OUTPUTS)
```
